# Optimizing a Trainium2 kernel written in Bass

```python
import jax, jax.numpy as jnp
from jax import lax
import numpy as np
import math

D_MODEL = 1024
BATCH = 1
SEQ = 512
DEPTH = 2

N_MIXERS = 2
PLE_DIM = 256
CONV_DIM = D_MODEL
CONV_WIDTH = 31
HEAD_DIM = 64
HEADS_PER_GROUP = 8
DILATION_GROUPS = ((128, 1), (512, 4), (2048, 16))
N_GROUPS = len(DILATION_GROUPS)
QKV_DIM = N_GROUPS * HEADS_PER_GROUP * HEAD_DIM
ATTN_OUT_DIM = HEADS_PER_GROUP * HEAD_DIM
BLOCK = 128
ROPE_THETA = 500000.0
ROT_DIM = HEAD_DIM // 4
EPS = 1e-6
NEG_INF = -1e30
N_CONV_LAYERS = (DEPTH + 1) // 2
N_ATTN_LAYERS = DEPTH // 2
OUT_SCALE = (2.0 * DEPTH) ** -0.5
PLE_SCALE = 0.5


def rms_norm(x, g):
    x32 = x.astype(jnp.float32)
    y = x32 * lax.rsqrt(jnp.mean(x32 * x32, axis=-1, keepdims=True) + EPS)
    return (y * g.astype(jnp.float32)).astype(x.dtype)

def layer_norm(x, g, b):
    x32 = x.astype(jnp.float32)
    xc = x32 - jnp.mean(x32, axis=-1, keepdims=True)
    y = xc * lax.rsqrt(jnp.mean(xc * xc, axis=-1, keepdims=True) + EPS)
    return (y * g.astype(jnp.float32) + b.astype(jnp.float32)).astype(x.dtype)

def rope_tables(positions):
    inv_freq = 1.0 / (ROPE_THETA ** (jnp.arange(0, ROT_DIM, 2, dtype=jnp.float32) / ROT_DIM))
    ang = positions.astype(jnp.float32)[..., None] * inv_freq
    return jnp.cos(ang), jnp.sin(ang)

def partial_rope(x, cos, sin):
    c = cos[:, :, None, None, :]
    s = sin[:, :, None, None, :]
    half = ROT_DIM // 2
    xr = x[..., :ROT_DIM].astype(jnp.float32)
    x1, x2 = xr[..., :half], xr[..., half:]
    rot = jnp.concatenate([x1 * c - x2 * s, x2 * c + x1 * s], axis=-1).astype(x.dtype)
    return jnp.concatenate([rot, x[..., ROT_DIM:]], axis=-1)

def dilated_band_attention(q, k, v, dilation, band):
    B, S, H, hd = q.shape
    L = S // dilation
    nb = -(-L // BLOCK)
    Lp = nb * BLOCK

    def to_blocks(t):
        t = t.reshape(B, L, dilation, H, hd).transpose(0, 2, 1, 3, 4)
        t = jnp.pad(t, ((0, 0), (0, 0), (0, Lp - L), (0, 0), (0, 0)))
        return t.reshape(B, dilation, nb, BLOCK, H, hd)

    def with_prev(t):
        prev = jnp.pad(t, ((0, 0), (0, 0), (1, 0), (0, 0), (0, 0), (0, 0)))[:, :, :-1]
        return jnp.concatenate([prev, t], axis=3)

    qb, kb, vb = to_blocks(q), to_blocks(k), to_blocks(v)
    kk, vv = with_prev(kb), with_prev(vb)
    s = jnp.einsum('bdnqhc,bdnkhc->bdnhqk', qb, kk,
                   preferred_element_type=jnp.float32) * (hd ** -0.5)
    qi = jnp.arange(BLOCK)[:, None]
    kj = jnp.arange(2 * BLOCK)[None, :]
    dist = BLOCK + qi - kj
    blk = jnp.arange(nb)[:, None, None]
    valid = (dist >= 0) & (dist <= band) & (blk * BLOCK + kj - BLOCK >= 0)
    s = jnp.where(valid[:, None], s, NEG_INF)
    m = jnp.max(s, axis=-1, keepdims=True)
    e = jnp.exp(s - m)
    den = jnp.sum(e, axis=-1, keepdims=True)
    probs = (e / den).astype(v.dtype)
    o = jnp.einsum('bdnhqk,bdnkhc->bdnqhc', probs, vv)
    lse = (m + jnp.log(den))[..., 0]
    o = o.reshape(B, dilation, Lp, H, hd)[:, :, :L].transpose(0, 2, 1, 3, 4).reshape(B, S, H, hd)
    lse = lse.transpose(0, 1, 2, 4, 3).reshape(B, dilation, Lp, H)[:, :, :L]
    lse = lse.transpose(0, 2, 1, 3).reshape(B, S, H)
    return o, lse

def conformer_conv_branch(h, w_in, dw, dw_b, ln_g, ln_b, w_out):
    u = h @ w_in
    a, b, gate = jnp.split(u, [CONV_DIM, 2 * CONV_DIM], axis=-1)
    y = a * jax.nn.sigmoid(b)
    y = lax.conv_general_dilated(
        y, dw[:, None, :].astype(y.dtype), window_strides=(1,),
        padding=((CONV_WIDTH - 1, 0),), dimension_numbers=('NWC', 'WIO', 'NWC'),
        feature_group_count=CONV_DIM) + dw_b
    y = layer_norm(y, ln_g, ln_b)
    y = jax.nn.silu(y) * jax.nn.silu(gate)
    return y @ w_out

def dilated_attention_branch(h, cos, sin, w_in, q_norm, k_norm, w_out):
    B, S, _ = h.shape
    u = h @ w_in
    q, k, v, gate = jnp.split(u, [QKV_DIM, 2 * QKV_DIM, 3 * QKV_DIM], axis=-1)
    shp = (B, S, N_GROUPS, HEADS_PER_GROUP, HEAD_DIM)
    q = partial_rope(rms_norm(q.reshape(shp), q_norm), cos, sin)
    k = partial_rope(rms_norm(k.reshape(shp), k_norm), cos, sin)
    v = v.reshape(shp)
    outs, lses = [], []
    for g, (window, dilation) in enumerate(DILATION_GROUPS):
        o, lse = dilated_band_attention(q[:, :, g], k[:, :, g], v[:, :, g], dilation, window // dilation)
        outs.append(o)
        lses.append(lse)
    wts = jax.nn.softmax(jnp.stack(lses, axis=0), axis=0)
    o = jnp.sum(wts[..., None] * jnp.stack(outs, axis=0).astype(jnp.float32), axis=0).astype(h.dtype)
    y = o.reshape(B, S, ATTN_OUT_DIM) * jax.nn.silu(gate)
    return y @ w_out

def first_inputs(seed: int = 0) -> dict:
    key = jax.random.key(seed)
    ks = jax.random.split(key, 20)
    f32 = jnp.float32
    nrm = lambda k, shape: jax.random.normal(k, shape, dtype=f32)
    x = nrm(ks[0], (BATCH, SEQ, D_MODEL))
    p = nrm(ks[1], (DEPTH, BATCH, SEQ, PLE_DIM))
    offsets = jax.random.randint(ks[2], (BATCH, 1), 0, 1024, dtype=jnp.int32)
    positions = (jnp.arange(SEQ, dtype=jnp.int32)[None, :] + offsets).astype(jnp.int32)
    norm_g = 1.0 + 0.02 * nrm(ks[3], (DEPTH, D_MODEL))
    conv_w_in = nrm(ks[4], (N_CONV_LAYERS, D_MODEL, 3 * CONV_DIM)) * D_MODEL ** -0.5
    conv_dw = nrm(ks[5], (N_CONV_LAYERS, CONV_WIDTH, CONV_DIM)) * CONV_WIDTH ** -0.5
    conv_dw_b = 0.02 * nrm(ks[6], (N_CONV_LAYERS, CONV_DIM))
    conv_ln_g = 1.0 + 0.02 * nrm(ks[7], (N_CONV_LAYERS, CONV_DIM))
    conv_ln_b = 0.02 * nrm(ks[8], (N_CONV_LAYERS, CONV_DIM))
    conv_w_out = nrm(ks[9], (N_CONV_LAYERS, CONV_DIM, D_MODEL)) * (CONV_DIM ** -0.5 * OUT_SCALE)
    attn_w_in = nrm(ks[10], (N_ATTN_LAYERS, D_MODEL, 3 * QKV_DIM + ATTN_OUT_DIM)) * D_MODEL ** -0.5
    attn_q_norm = 1.0 + 0.02 * nrm(ks[11], (N_ATTN_LAYERS, HEAD_DIM))
    attn_k_norm = 1.0 + 0.02 * nrm(ks[12], (N_ATTN_LAYERS, HEAD_DIM))
    attn_w_out = nrm(ks[13], (N_ATTN_LAYERS, ATTN_OUT_DIM, D_MODEL)) * (ATTN_OUT_DIM ** -0.5 * OUT_SCALE)
    ple_w_proj = nrm(ks[14], (DEPTH, PLE_DIM, D_MODEL)) * (PLE_DIM ** -0.5 * PLE_SCALE)
    ple_norm_g = 1.0 + 0.02 * nrm(ks[15], (DEPTH, D_MODEL))
    ple_w_gate = nrm(ks[16], (DEPTH, D_MODEL, D_MODEL)) * D_MODEL ** -0.5
    return {'x': x, 'p': p, 'positions': positions, 'norm_g': norm_g,
            'conv_w_in': conv_w_in, 'conv_dw': conv_dw, 'conv_dw_b': conv_dw_b,
            'conv_ln_g': conv_ln_g, 'conv_ln_b': conv_ln_b, 'conv_w_out': conv_w_out,
            'attn_w_in': attn_w_in, 'attn_q_norm': attn_q_norm, 'attn_k_norm': attn_k_norm,
            'attn_w_out': attn_w_out, 'ple_w_proj': ple_w_proj, 'ple_norm_g': ple_norm_g,
            'ple_w_gate': ple_w_gate}

def first_block(x, p, positions, norm_g, conv_w_in, conv_dw, conv_dw_b, conv_ln_g, conv_ln_b,
              conv_w_out, attn_w_in, attn_q_norm, attn_k_norm, attn_w_out, ple_w_proj,
              ple_norm_g, ple_w_gate):
    cos, sin = rope_tables(positions)
    for i in range(DEPTH):
        h = rms_norm(x, norm_g[i])
        j = i // N_MIXERS
        if i % N_MIXERS == 0:
            x = x + conformer_conv_branch(h, conv_w_in[j], conv_dw[j], conv_dw_b[j],
                                          conv_ln_g[j], conv_ln_b[j], conv_w_out[j])
        else:
            x = x + dilated_attention_branch(h, cos, sin, attn_w_in[j], attn_q_norm[j],
                                             attn_k_norm[j], attn_w_out[j])
        gate = jax.nn.sigmoid(rms_norm(x, ple_norm_g[i]) @ ple_w_gate[i])
        x = x + (p[i] @ ple_w_proj[i]) * gate
    return x


DEPTH_2 = 1

CHUNK = 64
ATT_HEADS = 8
ATT_KV_HEADS = 2
ATT_HEAD_DIM = 64
IDX_HEADS = 8
IDX_HEAD_DIM = 64
TOPK_MAX = 256
Q_BLOCK = 128
MLSTM_HEADS = 4
MLSTM_QK_DIM = 64
MLSTM_V_DIM = 128
CONV_WIDTH_2 = 4
MIX_A = ATT_HEADS * ATT_HEAD_DIM
MIX_B = MLSTM_HEADS * MLSTM_V_DIM
D_FF = 2816
SPLIT_WIDTHS = (
    ATT_HEADS * ATT_HEAD_DIM,
    ATT_KV_HEADS * ATT_HEAD_DIM,
    ATT_KV_HEADS * ATT_HEAD_DIM,
    IDX_HEADS * IDX_HEAD_DIM,
    IDX_HEAD_DIM,
    IDX_HEADS,
    MIX_B,
    MIX_B,
    MLSTM_HEADS,
    MLSTM_HEADS,
    MIX_B,
    D_MODEL,
    D_MODEL,
)
D_IN = sum(SPLIT_WIDTHS)


def rms_norm_2(x, g):
    xf = x.astype(jnp.float32)
    y = xf * lax.rsqrt(jnp.mean(xf * xf, axis=-1, keepdims=True) + EPS)
    return (y * g.astype(jnp.float32)).astype(x.dtype)

def swiglu_ffn(x, g, w_gate, w_up, w_down):
    h = rms_norm_2(x, g)
    return (jax.nn.silu(h @ w_gate) * (h @ w_up)) @ w_down

def split_columns(p):
    parts, off = [], 0
    for w in SPLIT_WIDTHS:
        parts.append(p[..., off:off + w])
        off += w
    return parts

def dsa_attention(q, k, v, iq, ik, iw):
    B, S = q.shape[0], q.shape[1]
    k_sel = min(TOPK_MAX, S // 4)
    nb = S // Q_BLOCK
    reps = ATT_HEADS // ATT_KV_HEADS
    idx_scale = (IDX_HEAD_DIM ** -0.5) * (IDX_HEADS ** -0.5)
    att_scale = ATT_HEAD_DIM ** -0.5
    key_pos = jnp.arange(S)

    qb = q.reshape(B, nb, Q_BLOCK, ATT_KV_HEADS, reps, ATT_HEAD_DIM).transpose(1, 0, 2, 3, 4, 5)
    iqb = iq.reshape(B, nb, Q_BLOCK, IDX_HEADS, IDX_HEAD_DIM).transpose(1, 0, 2, 3, 4)
    iwb = iw.reshape(B, nb, Q_BLOCK, IDX_HEADS).transpose(1, 0, 2, 3)
    ids = jnp.arange(nb, dtype=jnp.int32)

    def block(args):
        q_blk, iq_blk, iw_blk, bi = args
        t = bi * Q_BLOCK + jnp.arange(Q_BLOCK)
        logits = jnp.einsum('bqhd,bsd->bqhs', iq_blk, ik)
        score = jnp.einsum('bqhs,bqh->bqs', jax.nn.relu(logits), iw_blk).astype(jnp.float32) * idx_scale
        limit = (t // CHUNK + 1) * CHUNK
        allowed = key_pos[None, :] < limit[:, None]
        score = jnp.where(allowed[None], score, -jnp.inf)
        top_s, top_i = lax.top_k(score, k_sel)
        valid = jnp.isfinite(top_s)
        kg = jax.vmap(lambda kb, ib: kb[ib])(k, top_i)
        vg = jax.vmap(lambda vb, ib: vb[ib])(v, top_i)
        s = jnp.einsum('bqgrd,bqkgd->bqgrk', q_blk, kg).astype(jnp.float32) * att_scale
        s = jnp.where(valid[:, :, None, None, :], s, -jnp.inf)
        p = jax.nn.softmax(s, axis=-1).astype(vg.dtype)
        return jnp.einsum('bqgrk,bqkgd->bqgrd', p, vg)

    o = lax.map(block, (qb, iqb, iwb, ids))
    return o.transpose(1, 0, 2, 3, 4, 5).reshape(B, S, MIX_A)

def mlstm_branch(xm, vm, ig, fg, o_pre, conv_w, conv_b, w_mq, w_mk, b_i, b_f, head_g):
    B, S, _ = xm.shape
    H, L = MLSTM_HEADS, CHUNK
    nc = S // L
    xpad = jnp.pad(xm, ((0, 0), (CONV_WIDTH_2 - 1, 0), (0, 0)))
    xc = conv_b + xpad[:, 0:S] * conv_w[0]
    for j in range(1, CONV_WIDTH_2):
        xc = xc + xpad[:, j:j + S] * conv_w[j]
    xc = jax.nn.silu(xc).reshape(B, S, H, MLSTM_V_DIM)
    q = jnp.einsum('bshc,hcd->bshd', xc, w_mq).astype(jnp.float32) * (MLSTM_QK_DIM ** -0.5)
    k = jnp.einsum('bshc,hcd->bshd', xc, w_mk).astype(jnp.float32)
    v = vm.reshape(B, S, H, MLSTM_V_DIM).astype(jnp.float32)
    log_i = (ig + b_i).astype(jnp.float32)
    log_f = jax.nn.log_sigmoid((fg + b_f).astype(jnp.float32))

    def to_chunks(a):
        a = a.reshape((B, nc, L) + a.shape[2:])
        perm = (1, 0, 3, 2) + tuple(range(4, a.ndim))
        return a.transpose(perm)

    tril = jnp.tril(jnp.ones((L, L), dtype=bool))

    def step(carry, inp):
        C, n, m = carry
        qc, kc, vc, ic, fc = inp
        b = jnp.cumsum(fc, axis=-1)
        D = b[..., :, None] - b[..., None, :] + ic[..., None, :]
        D = jnp.where(tril, D, -jnp.inf)
        inter = b + m[..., None]
        m_t = jnp.maximum(jnp.max(D, axis=-1), inter)
        W = jnp.einsum('bhtd,bhsd->bhts', qc, kc) * jnp.exp(D - m_t[..., None])
        w_int = jnp.exp(inter - m_t)
        num = jnp.einsum('bhts,bhsv->bhtv', W, vc) + w_int[..., None] * jnp.einsum('bhtd,bhdv->bhtv', qc, C)
        den = jnp.sum(W, axis=-1) + w_int * jnp.einsum('bhtd,bhd->bht', qc, n)
        h = num / jnp.maximum(jnp.abs(den), jnp.exp(-m_t))[..., None]
        bL = b[..., -1]
        wk = bL[..., None] - b + ic
        m_new = jnp.maximum(bL + m, jnp.max(wk, axis=-1))
        ws = jnp.exp(wk - m_new[..., None])
        wc = jnp.exp(bL + m - m_new)
        C_new = wc[..., None, None] * C + jnp.einsum('bhs,bhsd,bhsv->bhdv', ws, kc, vc)
        n_new = wc[..., None] * n + jnp.einsum('bhs,bhsd->bhd', ws, kc)
        return (C_new, n_new, m_new), h

    init = (jnp.zeros((B, H, MLSTM_QK_DIM, MLSTM_V_DIM), jnp.float32),
            jnp.zeros((B, H, MLSTM_QK_DIM), jnp.float32),
            jnp.zeros((B, H), jnp.float32))
    _, hs = lax.scan(step, init, (to_chunks(q), to_chunks(k), to_chunks(v), to_chunks(log_i), to_chunks(log_f)))
    h = hs.transpose(1, 0, 3, 2, 4).reshape(B, S, H, MLSTM_V_DIM)
    h = rms_norm_2(h, head_g.reshape(H, MLSTM_V_DIM)).reshape(B, S, MIX_B).astype(xm.dtype)
    return h * jax.nn.sigmoid(o_pre)

def second_inputs(seed: int = 0) -> dict:
    key = jax.random.key(seed)
    ks = jax.random.split(key, 32)
    f32 = jnp.float32

    def nrm(k, shape, fan_in):
        return jax.random.normal(k, shape, f32) * (fan_in ** -0.5)

    def gain(k, shape):
        return 1.0 + 0.02 * jax.random.normal(k, shape, f32)

    Ld = DEPTH_2
    return {
        "x": jax.random.normal(ks[0], (BATCH, SEQ, D_MODEL), f32),
        "ffn1_norm": gain(ks[1], (Ld, D_MODEL)),
        "ffn1_w_gate": nrm(ks[2], (Ld, D_MODEL, D_FF), D_MODEL),
        "ffn1_w_up": nrm(ks[3], (Ld, D_MODEL, D_FF), D_MODEL),
        "ffn1_w_down": nrm(ks[4], (Ld, D_FF, D_MODEL), D_FF),
        "mix_norm": gain(ks[5], (Ld, D_MODEL)),
        "w_in": nrm(ks[6], (Ld, D_MODEL, D_IN), D_MODEL),
        "q_norm": gain(ks[7], (Ld, ATT_HEAD_DIM)),
        "k_norm": gain(ks[8], (Ld, ATT_HEAD_DIM)),
        "idx_k_norm": gain(ks[9], (Ld, IDX_HEAD_DIM)),
        "conv_w": nrm(ks[10], (Ld, CONV_WIDTH_2, MIX_B), CONV_WIDTH_2),
        "conv_b": 0.02 * jax.random.normal(ks[11], (Ld, MIX_B), f32),
        "w_mq": nrm(ks[12], (Ld, MLSTM_HEADS, MLSTM_V_DIM, MLSTM_QK_DIM), MLSTM_V_DIM),
        "w_mk": nrm(ks[13], (Ld, MLSTM_HEADS, MLSTM_V_DIM, MLSTM_QK_DIM), MLSTM_V_DIM),
        "b_i": 0.1 * jax.random.normal(ks[14], (Ld, MLSTM_HEADS), f32),
        "b_f": 3.0 + 0.1 * jax.random.normal(ks[15], (Ld, MLSTM_HEADS), f32),
        "m_head_norm": gain(ks[16], (Ld, MIX_B)),
        "w_proj_a": nrm(ks[17], (Ld, MIX_A, D_MODEL), MIX_A),
        "w_proj_b": nrm(ks[18], (Ld, MIX_B, D_MODEL), MIX_B),
        "w_out": nrm(ks[19], (Ld, D_MODEL, D_MODEL), D_MODEL),
        "ffn2_norm": gain(ks[20], (Ld, D_MODEL)),
        "ffn2_w_gate": nrm(ks[21], (Ld, D_MODEL, D_FF), D_MODEL),
        "ffn2_w_up": nrm(ks[22], (Ld, D_MODEL, D_FF), D_MODEL),
        "ffn2_w_down": nrm(ks[23], (Ld, D_FF, D_MODEL), D_FF),
    }

def second_block(x, ffn1_norm, ffn1_w_gate, ffn1_w_up, ffn1_w_down, mix_norm, w_in,
              q_norm, k_norm, idx_k_norm, conv_w, conv_b, w_mq, w_mk, b_i, b_f,
              m_head_norm, w_proj_a, w_proj_b, w_out, ffn2_norm, ffn2_w_gate,
              ffn2_w_up, ffn2_w_down):
    B, S, _ = x.shape
    for l in range(DEPTH_2):
        x = x + 0.5 * swiglu_ffn(x, ffn1_norm[l], ffn1_w_gate[l], ffn1_w_up[l], ffn1_w_down[l])
        h = rms_norm_2(x, mix_norm[l])
        (aq, ak, av, iq, ik, iw, mx, mv, mi, mf, mo, ga, gb) = split_columns(h @ w_in[l])
        q = rms_norm_2(aq.reshape(B, S, ATT_HEADS, ATT_HEAD_DIM), q_norm[l])
        k = rms_norm_2(ak.reshape(B, S, ATT_KV_HEADS, ATT_HEAD_DIM), k_norm[l])
        v = av.reshape(B, S, ATT_KV_HEADS, ATT_HEAD_DIM)
        iq = iq.reshape(B, S, IDX_HEADS, IDX_HEAD_DIM)
        ik = rms_norm_2(ik, idx_k_norm[l])
        ya = dsa_attention(q, k, v, iq, ik, iw)
        yb = mlstm_branch(mx, mv, mi, mf, mo, conv_w[l], conv_b[l], w_mq[l], w_mk[l],
                          b_i[l], b_f[l], m_head_norm[l])
        merged = jax.nn.sigmoid(ga) * (ya @ w_proj_a[l]) + jax.nn.sigmoid(gb) * (yb @ w_proj_b[l])
        x = x + merged @ w_out[l]
        x = x + 0.5 * swiglu_ffn(x, ffn2_norm[l], ffn2_w_gate[l], ffn2_w_up[l], ffn2_w_down[l])
    return x


def setup_inputs(seed=0):
    out = dict(first_inputs(seed))
    for name, value in second_inputs(seed + 1).items():
        if name != "x":
            out[name + "_2"] = value
    return out


def reference(
    x, p, positions, norm_g, conv_w_in, conv_dw, conv_dw_b, conv_ln_g, conv_ln_b, conv_w_out,
    attn_w_in, attn_q_norm, attn_k_norm, attn_w_out, ple_w_proj, ple_norm_g, ple_w_gate,
    ffn1_norm_2, ffn1_w_gate_2, ffn1_w_up_2, ffn1_w_down_2, mix_norm_2, w_in_2, q_norm_2,
    k_norm_2, idx_k_norm_2, conv_w_2, conv_b_2, w_mq_2, w_mk_2, b_i_2, b_f_2, m_head_norm_2,
    w_proj_a_2, w_proj_b_2, w_out_2, ffn2_norm_2, ffn2_w_gate_2, ffn2_w_up_2, ffn2_w_down_2,
):
    x = first_block(
        x, p, positions, norm_g, conv_w_in, conv_dw, conv_dw_b, conv_ln_g, conv_ln_b,
        conv_w_out, attn_w_in, attn_q_norm, attn_k_norm, attn_w_out, ple_w_proj, ple_norm_g,
        ple_w_gate,
    )
    return second_block(
        x, ffn1_norm_2, ffn1_w_gate_2, ffn1_w_up_2, ffn1_w_down_2, mix_norm_2, w_in_2, q_norm_2,
        k_norm_2, idx_k_norm_2, conv_w_2, conv_b_2, w_mq_2, w_mk_2, b_i_2, b_f_2, m_head_norm_2,
        w_proj_a_2, w_proj_b_2, w_out_2, ffn2_norm_2, ffn2_w_gate_2, ffn2_w_up_2, ffn2_w_down_2,
    )


_drawn_inputs = setup_inputs


def setup_inputs(seed=0):
    import zlib

    import numpy as np

    out = dict(_drawn_inputs(seed))
    spreads = {}
    factors = {'norm_g': 7.191,
     'conv_dw_b': 5.406,
     'conv_ln_g': 8.0,
     'conv_ln_b': 8.0,
     'attn_q_norm': 8.0,
     'attn_k_norm': 8.0,
     'ple_norm_g': 33.731,
     'ffn1_norm_2': 5.276,
     'mix_norm_2': 3.849,
     'q_norm_2': 94.389,
     'k_norm_2': 92.637,
     'idx_k_norm_2': 112.232,
     'conv_b_2': 28.871,
     'b_i_2': 200.0,
     'b_f_2': 39.472,
     'm_head_norm_2': 64.0,
     'ffn2_norm_2': 23.702}
    for name, (base, spread) in spreads.items():
        noise = np.random.default_rng([zlib.crc32(name.encode()), seed]).standard_normal(out[name].shape)
        drawn = base * np.exp(spread * noise) if base else spread * noise
        out[name] = __import__('jax').numpy.asarray(drawn.astype(out[name].dtype))
    for name, factor in factors.items():
        out[name] = (out[name] * factor).astype(out[name].dtype)
    return out
```

```python
from collections import defaultdict
from contextlib import ExitStack, contextmanager

import numpy as np

import concourse.bass as bass
from concourse import mybir

P = 128
S = 512
D = 1024
KC = D // P
RING = 4
AHEAD = 2
EPS = 1e-6
NEG = -1e30
TAKEN = -3e38
CONV_W = 31
D_FF = 2816
FF = D_FF // P
HEAD = 64
GROUPS = 3
TOPK = 128
MH = 4
NQ = S // P

F32 = mybir.dt.float32
F32R = mybir.dt.float32r
I32 = mybir.dt.int32
ALU = mybir.AluOpType
ACT = mybir.ActivationFunctionType
AX = mybir.AxisListType

PARAMS = {}
_at = 0
for _name, _n in (("norm_g0", 8), ("norm_g1", 8), ("ple_g0", 8), ("ple_g1", 8), ("taps", 8 * 32), ("ln_g", 8),
                  ("ln_b", 8), ("q_norm", 1), ("k_norm", 1), ("ffn1", 8), ("mix", 8), ("q_norm2", 1),
                  ("k_norm2", 1), ("idx_norm", 1), ("conv2", 4 * 4), ("conv2_b", 4), ("m_head", 4), ("ffn2", 8),
                  ("b_i", 1), ("b_f", 1), ("inv_freq", 1), ("eps", 1), ("w_mq", 4 * 64), ("w_mk", 4 * 64)):
    PARAMS[_name] = _at
    _at += _n
NPARAM = _at

CONSTS = {"ident": 0, "ones": 128, "head_ones": 256, "rot": 384, "diag_block": 512, "diag_causal": 640,
          "pick": 768}
NCONST = 768 + 4 * P

N_TILES = 24 + 8 + 10 + 40 + 4 + 10 + (2 * FF + 24) + 40 + 8 + 8 + (2 * FF + 24)


READS = (16, 8, 10, 40, 4, 10, FF, 8, 13, 11, 8, 8, FF, 8)
TILES = (24, 8, 10, 40, 4, 10, 2 * FF, 24, 13, 11, 24, 8, 2 * FF, 24)
TILES0 = [0] + [sum(TILES[:n]) for n in range(14)]
READ0 = [0] + [4 + sum(READS[:n]) for n in range(14)]
RAW = range(6)
PI = 3.1415925
ROUND = 1.5 * 2.0 ** 23
TURN = (6.28125, 0.0019350051879882812, 3.019916e-07)


class Counts:

    def __init__(self):
        self.n, self.rate, self.i = defaultdict(int), {}, None

    def at(self, sem, off=0):
        v = self.n.get(sem, 0) + off
        if self.i is not None and self.rate.get(sem, 0):
            return self.i * self.rate[sem] + v
        return v

    def up(self, sem, by=1):
        self.n[sem] = self.n.get(sem, 0) + by
        return self.at(sem)

    @contextmanager
    def repeat(self, eng, times, rates):
        before = dict(self.n)
        self.rate = rates
        with eng.Fori(0, times) as i:
            self.i = i
            yield i
        self.i = None
        made = {s: v - before.get(s, 0) for s, v in self.n.items() if v != before.get(s, 0)}
        if made != {s: r for s, r in rates.items() if r}:
            raise ValueError("rates: " + str({(s if isinstance(s, str) else s.name): r for s, r in made.items()}))
        for s, r in made.items():
            self.n[s] = before.get(s, 0) + r * times


def build(nc, weights, x_in, ple_in, pos_in, params_in, consts_in, masks_in, out, stop=99):
    ctx = ExitStack()
    with ctx:
        def sb(name, shape, dt=F32):
            return ctx.enter_context(nc.sbuf_tensor(name, shape, dt))

        def sem(name):
            return ctx.enter_context(nc.semaphore(name))

        X = sb("X", [P, KC, S])
        H_hi = sb("H_hi", [P, KC, S], F32R)
        H_lo = sb("H_lo", [P, KC, S], F32R)
        w_raw = sb("w_raw", [P, RING, D])
        w_hi = sb("w_hi", [P, RING, D], F32R)
        w_lo = sb("w_lo", [P, RING, D], F32R)
        par = sb("par", [P, NPARAM])
        con = sb("con", [P, NCONST])
        sq = sb("sq", [P, 2, S])
        tmp = sb("tmp", [P, 2, S])
        var = sb("var", [P, S])
        r0 = sb("r0", [P, S])
        rs = sb("rs", [P, S])
        ps = ctx.enter_context(nc.psum_tensor("ps", [P, 8, S], F32))

        def const(name, n=P):
            return con[:, CONSTS[name]:CONSTS[name] + n]

        def col(name, j=0, n=1):
            return par[:, PARAMS[name] + j:PARAMS[name] + j + n]

        ident = const("ident")
        ones = const("ones")
        head_ones = const("head_ones")

        def scope(*specs):
            with ExitStack() as s:
                return [s.enter_context(nc.sbuf_tensor(n, sh, dt)) for n, sh, dt in specs]

        cv_sg, cv_a, cv_acc, cv_w, cv_Y, cv_G = scope(
            ("cv_sg", [P, 2, S], F32), ("cv_a", [P, 2, S], F32), ("cv_acc", [P, 2, S], F32),
            ("cv_w", [P, 2, 32], F32), ("cv_Y", [P, KC, S], F32), ("cv_G", [P, KC, S], F32))
        pl_raw, pl_hi, pl_lo, pl_P = scope(
            ("pl_raw", [P, 2, S], F32), ("pl_hi", [P, 2, S], F32R), ("pl_lo", [P, 2, S], F32R),
            ("pl_P", [P, KC, S], F32))
        (at_mask, at_C, at_S, at_G, at_raw, at_ab, at_vT, at_V, at_SG, at_Sm, at_PT, at_st, at_var,
         at_r0, at_Yh, at_Yl) = scope(
            ("at_mask", [P, 4, 768], F32), ("at_C", [P, S], F32), ("at_S", [P, S], F32),
            ("at_G", [P, 4, P], F32), ("at_raw", [P, 6, S], F32), ("at_ab", [P, 4, S], F32), ("at_vT", [P, 3, S], F32), ("at_V", [P, 3, S], F32),
            ("at_SG", [P, S], F32), ("at_Sm", [P, 2, 768], F32), ("at_PT", [P, 768], F32),
            ("at_st", [P, 8, 4], F32), ("at_var", [P, 2, S], F32), ("at_r0", [P, 2, S], F32), ("at_Yh", [P, 4, S], F32R), ("at_Yl", [P, 4, S], F32R))
        mid_hi, mid_lo = scope(("mid_hi", [P, FF, S], F32R), ("mid_lo", [P, FF, S], F32R))
        with ExitStack() as s_mix:
            def keep(n, sh, dt):
                return s_mix.enter_context(nc.sbuf_tensor(n, sh, dt))
            yb_hi, yb_lo = keep("yb_hi", [P, 4, S], F32R), keep("yb_lo", [P, 4, S], F32R)
            IW = keep("IW", [P, NQ, 8], F32)
            (ml_U, ml_sm, ml_g, ml_c, ml_m, ml_xc, ml_q, ml_k, ml_V, ml_NM, ml_NMd, ml_E, ml_W, ml_cT,
             ml_h, ml_EB) = scope(
                ("ml_U", [P, 12, S], F32), ("ml_sm", [P, S], F32), ("ml_g", [4, 4, S], F32),
                ("ml_c", [4, S], F32), ("ml_m", [4, 2, S], F32), ("ml_xc", [P, S], F32),
                ("ml_q", [HEAD, S], F32), ("ml_k", [HEAD, S], F32), ("ml_V", [P, NQ, P], F32),
                ("ml_NM", [P, S], F32), ("ml_NMd", [P, NQ, P], F32), ("ml_E", [P, S], F32),
                ("ml_W", [P, S], F32), ("ml_cT", [P, NQ, 4], F32), ("ml_h", [P, S], F32),
                ("ml_EB", [P, S], F32))
            ya_hi, ya_lo = keep("ya_hi", [P, 4, S], F32R), keep("ya_lo", [P, 4, S], F32R)
            (ds_U, ds_kvi, ds_V, ds_acc, ds_bias, ds_P, ds_PT, ds_st, ds_mx) = scope(
                ("ds_U", [P, 8, S], F32), ("ds_kvi", [P, 3, S], F32), ("ds_V", [P, NQ, P], F32),
                ("ds_acc", [P, S], F32), ("ds_bias", [P, NQ, S], F32), ("ds_P", [P, 2, S], F32),
                ("ds_PT", [P, 2, S], F32), ("ds_st", [P, 32, 4], F32), ("ds_mx", [P, 8], F32))
            mg_s, mg_t, m_hi, m_lo = scope(
                ("mg_s", [P, 4, S], F32), ("mg_t", [P, 2, S], F32), ("m_hi", [P, KC, S], F32R),
                ("m_lo", [P, KC, S], F32R))

        landed = [sem(f"landed{i}") for i in range(RING)]
        x_loaded, par_loaded, con_loaded, ple_loaded, mask_loaded, pos_loaded = (sem(n) for n in (
            "x_loaded", "par_loaded", "con_loaded", "ple_loaded", "mask_loaded", "pos_loaded"))
        stored = sem("stored")
        hi_done = sem("hi_done")
        lo_done = sem("lo_done")
        tile_done = sem("tile_done")
        read_out = sem("read_out")
        ended = {e: sem(f"ended_{e}") for e in ("act", "dve", "pe", "pool")}
        act_chain = sem("act_chain")
        dve_chain = sem("dve_chain")
        gated = sem("gated")
        sq_done = sem("sq_done")
        sq_used = sem("sq_used")
        r0_done = sem("r0_done")
        rs_done = sem("rs_done")
        tmp_done = sem("tmp_done")
        split_hi = sem("split_hi")
        split_lo = sem("split_lo")
        act_out = sem("act_out")
        dve_out = sem("dve_out")
        pe_out = sem("pe_out")
        pool_out = sem("pool_out")
        rot_done = sem("rot_done")
        n_done = sem("n_done")
        s_done = sem("s_done")
        m_done = sem("m_done")
        e_done = sem("e_done")
        p_done = sem("p_done")
        t_done = sem("t_done")
        pt_done = sem("pt_done")
        o_done = sem("o_done")

        block = ctx.enter_context(nc.Block())

        NSTAGES = min(stop, 14)
        N_ENDS = NSTAGES + (5 if NSTAGES >= 4 else 0)
        followed = {}

        def begin(k, stage):
            k.n[tile_done], k.n[read_out] = TILES0[stage], READ0[stage]

        def stage_end(eng, own, k, stage=None):
            if stage is not None:
                for s, v in k.n.items():
                    if v and s not in (tile_done, read_out, "prep", "tile") and s not in landed:
                        if followed.setdefault((stage, s), v) != v:
                            raise ValueError(f"stage {stage}, {own}: {s.name} {v}, others {followed[stage, s]}")
            eng.drain().then_inc(ended[own], 1)
            k.up(ended[own])
            for other in ended:
                if other != own:
                    eng.wait_ge(ended[other], k.up(ended[other]))

        def DSA_NORMED(u, kvi):
            return [(u[:, c, :], "q_norm2") for c in range(4)] + [(kvi[:, 0, :], "k_norm2"), (kvi[:, 2, :], "idx_norm")]

        def bank_of(tile):
            return tile % 4

        def chunk(t, j):
            return t[:, bass.ds(j, 1), :]

        def flat(ap):
            return ap.rearrange("p a b -> p (a b)")

        @block.sync
        def _(sp):
            for u in range(RING):
                sp.dma_start(w_raw[:, u, :], weights[u]).then_inc(landed[u], 16)
            n_tiles = sum(TILES[:NSTAGES])
            with sp.Fori(1, n_tiles // RING) as i:
                for u in range(RING):
                    sp.wait_ge(lo_done, RING * i + u - RING + 1)
                    sp.dma_start(w_raw[:, u, :], weights[RING * i + u]).then_inc(landed[u], 16)
            for n in range(n_tiles // RING * RING, n_tiles + AHEAD):
                sp.wait_ge(lo_done, n - RING + 1)
                sp.dma_start(w_raw[:, n % RING, :], weights[n % N_TILES]).then_inc(landed[n % RING], 16)
            sp.wait_ge(ended["dve"], N_ENDS)
            sp.dma_start(out, X[:, :, :]).then_inc(stored, 16)
            sp.wait_ge(stored, 16)

        @block.gpsimd
        def _(pool):
            k = Counts()

            def rotation_products():
                for j in range(6):
                    pool.wait_ge(read_out, k.up(read_out, 10) if j == 0 else k.at(read_out))
                    if j >= 2:
                        pool.wait_ge(rot_done, k.up(rot_done))
                    for n, table in enumerate((at_C, at_S)):
                        pool.tensor_tensor(at_ab[:, 2 * (j % 2) + n, :], at_raw[:, RAW[j], :], table[:, :],
                                           ALU.mult).then_inc(pool_out, 1)
                k.up(rot_done, 2)

            for stage in range(1, NSTAGES + 1):
                if stage == 4:
                    begin(k, 4)
                    pool.dma_start(at_SG[:, :].bitcast(I32), pos_in.to_broadcast([P, S])).then_inc(pos_loaded, 16)
                    stage_end(pool, "pool", k)
                    with k.repeat(pool, 2, {read_out: 20, rot_done: 12, **{e: 2 for e in ended.values()}}):
                        for _ in range(2):
                            rotation_products()
                            stage_end(pool, "pool", k)
                stage_end(pool, "pool", k, stage)

        @block.scalar
        def _(act):
            k = Counts()

            def link(instr):
                instr.then_inc(act_chain, 1)
                act.wait_ge(act_chain, k.up(act_chain))

            def copy(out_ap, in_ap):
                return act.activation(out_ap, in_ap, ACT.Copy)

            def prep():
                n = k.n.get("prep", 0)
                s = n % RING
                act.wait_ge(landed[s], k.up(landed[s], 16))
                if n >= RING:
                    act.wait_ge(tile_done, k.at("prep", 1 - RING))
                copy(w_hi[:, s, :], w_raw[:, s, :]).then_inc(hi_done, 1)
                k.up("prep")

            def prep_rates(tiles, **more):
                return {"prep": tiles, **{landed[s]: 4 * tiles for s in range(RING)}}

            def square(src):
                n = k.n.get(sq_done, 0)
                if n >= 2:
                    act.wait_ge(sq_used, k.at(sq_done, -1))
                act.activation(sq[:, n % 2, :], src, ACT.Square).then_inc(sq_done, 1)
                k.up(sq_done)

            def guess(bank, scale, var_ap, r0_ap, behind=1, squares=0):
                act.wait_ge(sq_used, k.at(sq_done, -squares))
                if k.n.get(r0_done, 0) >= behind:
                    act.wait_ge(rs_done, k.at(r0_done, 1 - behind))
                link(act.activation(var_ap, ps[:, bank, :], ACT.Identity, bias=col("eps"), scale=scale))
                link(act.activation(r0_ap, var_ap, ACT.Ln))
                act.activation(r0_ap, r0_ap, ACT.Exp, scale=-0.5).then_inc(r0_done, 1)
                k.up(r0_done)

            def split(dst, src_slot=None, src=None):
                act.wait_ge(tmp_done, k.up(tmp_done))
                copy(dst, tmp[:, src_slot, :] if src is None else src).then_inc(split_hi, 1)
                k.up(split_hi)

            def norm(src, scale=1.0 / D, apply=True):
                for c in range(KC):
                    square(src[:, c, :])
                guess(4, scale, var[:, :], r0[:, :])
                for c in range(KC if apply else 0):
                    split(H_hi[:, c, :], c % 2)

            def ple():
                act.wait_ge(ple_loaded, k.up(ple_loaded, 16))
                copy(pl_hi[:, :, :], pl_raw[:, :, :]).then_inc(act_out, 1)
                k.up(act_out)
                k.up(dve_out)
                for half in range(2):
                    prep()
                    act.wait_ge(tile_done, k.up(tile_done))
                    copy(pl_P[:, 4 * half:4 * half + 4, :], ps[:, 0:4, :]).then_inc(read_out, 1)
                    k.up(read_out)
                    if half == 0:
                        norm(X)
                with k.repeat(act, 2, {tile_done: 4, gated: 4, read_out: 4, **prep_rates(4)}):
                    for u in range(4):
                        prep()
                        act.wait_ge(tile_done, k.up(tile_done))
                        act.wait_ge(read_out, k.at(read_out, -1))
                        k.up(read_out)
                        act.activation(sq[:, u % 2, :], ps[:, bank_of(k.n["prep"] - AHEAD - 1), :], ACT.Sigmoid)\
                            .then_inc(gated, 1)
                        k.up(gated)

            def adds_to_x(tiles, body):
                with k.repeat(act, tiles // body, {**prep_rates(body)}):
                    for u in range(body):
                        prep()

            def ffn_up():
                norm(X)
                with k.repeat(act, FF // 2, {tile_done: 4, read_out: 2, gated: 2, split_hi: 2,
                                                    **prep_rates(4)}) as i:
                    for j in range(2):
                        for u in range(2):
                            prep()
                            act.wait_ge(tile_done, k.up(tile_done))
                            if u == 0:
                                act.wait_ge(read_out, k.at(read_out, -1))
                                k.up(read_out)
                                act.activation(sq[:, j, :], ps[:, bank_of(k.n["prep"] - AHEAD - 1), :], ACT.Silu)\
                                    .then_inc(gated, 1)
                                k.up(gated)
                        act.wait_ge(read_out, k.at(read_out))
                        copy(chunk(mid_hi, 2 * i + j), tmp[:, j:j + 1, :]).then_inc(split_hi, 1)
                        k.up(split_hi)

            act.dma_start(X[:, :, :], x_in).then_inc(x_loaded, 16)
            act.dma_start(par[:, :], params_in).then_inc(par_loaded, 16)
            act.dma_start(con[:, :], consts_in).then_inc(con_loaded, 16)
            act.wait_ge(x_loaded, 16)
            act.wait_ge(par_loaded, 16)
            for _ in range(AHEAD):
                prep()
            begin(k, 1)
            norm(X)
            with k.repeat(act, 4, {tile_done: 4, gated: 2, read_out: 2, **prep_rates(4)}):
                for j in range(2):
                    for u in range(2):
                        prep()
                        act.wait_ge(tile_done, k.up(tile_done))
                    act.wait_ge(read_out, k.at(read_out, -1))
                    k.up(read_out)
                    act.activation(cv_sg[:, j, :], ps[:, 2 * j + 1, :], ACT.Sigmoid).then_inc(gated, 1)
                    k.up(gated)
            with k.repeat(act, 2, {tile_done: 4, read_out: 4, **prep_rates(4)}) as i:
                for u in range(4):
                    prep()
                    act.wait_ge(tile_done, k.up(tile_done))
                    act.activation(chunk(cv_G, 4 * i + u), ps[:, u:u + 1, :], ACT.Silu).then_inc(read_out, 1)
                    k.up(read_out)
            stage_end(act, "act", k, 1)
            if NSTAGES >= 2:
                begin(k, 2)
                k.up(pe_out)
                for c in range(KC):
                    act.wait_ge(n_done, k.up(n_done))
                    square(cv_Y[:, c, :])
                guess(4, 1.0 / D, var[:, :], r0[:, :])
                for c in range(KC):
                    act.wait_ge(tmp_done, k.up(tmp_done))
                    act.activation(sq[:, c % 2, :], tmp[:, c % 2, :], ACT.Silu, bias=col("ln_b", c)).then_inc(act_out, 1)
                    k.up(act_out)
                    split(H_hi[:, c, :], src=cv_Y[:, c, :])
                adds_to_x(8, 4)
                stage_end(act, "act", k, 2)
            if NSTAGES >= 3:
                begin(k, 3)
                act.dma_start(pl_raw[:, :, :], ple_in[0]).then_inc(ple_loaded, 16)
                ple()
                stage_end(act, "act", k, 3)
            if NSTAGES >= 4:
                begin(k, 4)
                act.dma_start(at_mask[:, :, :], masks_in).then_inc(mask_loaded, 16)
                act.wait_ge(dve_out, k.up(dve_out))
                link(act.activation(at_S[:, :], at_C[:, :], ACT.Sin))
                act.activation(at_C[:, :], at_SG[:, :], ACT.Sin).then_inc(act_out, 1)
                k.up(act_out)
                norm(X)
                stage_end(act, "act", k)
                rates = {tile_done: 20, read_out: 20, n_done: 12, sq_done: 12, r0_done: 12, act_chain: 24, act_out: 2,
                         **{s: 16 for s in (m_done, e_done, pt_done, t_done)}, o_done: 16, pe_out: 2,
                         tmp_done: 2, split_hi: 2, rs_done: 0, **{e: 2 for e in ended.values()}, **prep_rates(20)}
                with k.repeat(act, 2, rates) as i:
                    for cc in range(2):
                        for j in range(10):
                            prep()
                            act.wait_ge(tile_done, k.up(tile_done))
                            src = ps[:, bank_of(k.n["prep"] - AHEAD - 1), :]
                            if j == 9:
                                act.activation(at_SG[:, :], src, ACT.Silu).then_inc(read_out, 1)
                            elif j % 3 == 2:
                                copy(at_vT[:, j // 3, :], src).then_inc(read_out, 1)
                            else:
                                copy(at_raw[:, 2 * (j // 3) + j % 3, :], src).then_inc(read_out, 1)
                            k.up(read_out)
                        act.wait_ge(pe_out, k.up(pe_out))
                        copy(at_V[:, :, :], ps[:, 0:3, :]).then_inc(act_out, 1)
                        k.up(act_out)
                        act.wait_ge(read_out, k.at(read_out))
                        square(at_raw[:, 0, :])
                        k.up(n_done, 6)
                        for j in range(6):
                            if j < 5:
                                square(at_raw[:, j + 1, :])
                            guess(4 + j % 2, 1.0 / HEAD, at_var[:, j % 2, :], at_r0[:, j % 2, :], behind=2,
                                  squares=j < 5)

                        def exps(u):
                            act.wait_ge(m_done, k.up(m_done))
                            act.activation(at_Sm[:, u % 2, :], at_Sm[:, u % 2, :], ACT.Exp, bias=at_st[:, u, 1:2],
                                           accum_out=at_st[:, u, 2:3]).then_inc(e_done, 1)
                            k.up(e_done)

                        exps(0)
                        for u in range(8):
                            if u < 7:
                                exps(u + 1)
                            act.wait_ge(t_done, k.up(t_done))
                            copy(at_PT[:, :], flat(ps[:, 0:2, :])[:, 0:768]).then_inc(pt_done, 1)
                            k.up(pt_done)
                        k.up(o_done, 8)
                        act.wait_ge(tmp_done, k.up(tmp_done))
                        copy(chunk(at_Yh, 2 * i + cc), tmp[:, cc:cc + 1, :]).then_inc(split_hi, 1)
                        k.up(split_hi)
                        stage_end(act, "act", k)
                stage_end(act, "act", k, 4)
            if NSTAGES >= 5:
                begin(k, 5)
                for _ in range(4):
                    prep()
                stage_end(act, "act", k, 5)
            if NSTAGES >= 6:
                begin(k, 6)
                act.dma_start(pl_raw[:, :, :], ple_in[1]).then_inc(ple_loaded, 16)
                ple()
                stage_end(act, "act", k, 6)
            if NSTAGES >= 7:
                begin(k, 7)
                ffn_up()
                stage_end(act, "act", k, 7)
            if NSTAGES >= 8:
                begin(k, 8)
                adds_to_x(24, 12)
                stage_end(act, "act", k, 8)
            if NSTAGES >= 9:
                begin(k, 9)
                norm(X)
                with k.repeat(act, 3, {tile_done: 4, read_out: 4, **prep_rates(4)}) as i:
                    for u in range(4):
                        prep()
                        act.wait_ge(tile_done, k.up(tile_done))
                        b = bank_of(k.n["prep"] - AHEAD - 1)
                        copy(chunk(ml_U, 4 * i + u), ps[:, b:b + 1, :]).then_inc(read_out, 1)
                        k.up(read_out)
                prep()
                act.wait_ge(tile_done, k.up(tile_done))
                copy(ml_sm[:, :], ps[:, bank_of(k.n["prep"] - AHEAD - 1), :]).then_inc(read_out, 1)
                act.wait_ge(read_out, k.up(read_out))
                act.wait_ge(pe_out, k.up(pe_out))
                act.activation(IW[:, :, :], ps[:, 4, :].rearrange("p (b r) -> p b r", r=P)[:, :, 0:8], ACT.Copy,
                               scale=(HEAD ** -0.5) * (8 ** -0.5)).then_inc(act_out, 1)
                k.up(act_out)
                act.wait_ge(dve_out, k.up(dve_out))
                link(act.activation(ml_m[:, 0, :], ml_g[:, 1, :], ACT.Abs))
                link(act.activation(ml_m[:, 0, :], ml_m[:, 0, :], ACT.Exp, scale=-1.0))
                act.activation(ml_m[:, 0, :], ml_m[:, 0, :], ACT.Ln, bias=1.0).then_inc(act_out, 1)
                k.up(act_out)
                k.up(dve_out)
                act.wait_ge(pe_out, k.up(pe_out))
                copy(ml_cT[:, :, :], ps[:, 5, 0:16].rearrange("p (b h) -> p b h", h=4)).then_inc(act_out, 1)
                k.up(act_out)
                for h in range(MH):
                    act.wait_ge(dve_out, k.up(dve_out))
                    act.activation(ml_xc[:, :], ml_h[:, :], ACT.Silu).then_inc(act_out, 1)
                    k.up(act_out)
                    act.wait_ge(pe_out, k.up(pe_out))
                    copy(ml_q[:, :], ps[0:HEAD, 4, :])
                    copy(ml_k[:, :], ps[0:HEAD, 5, :])
                    copy(ml_NM[:, :], ps[:, 6, :])
                    copy(ml_V[:, :, :], ps[:, 0, :].rearrange("p (b v) -> p b v", v=P))
                    act.activation(ml_EB[:, :], ps[:, 7, :], ACT.Exp).then_inc(act_out, 1)
                    act.wait_ge(act_out, k.up(act_out))
                    act.wait_ge(dve_out, k.up(dve_out))
                    for b in range(NQ):
                        if b:
                            act.wait_ge(dve_out, k.up(dve_out))
                        n = S - P * b
                        last = act.activation(ml_E[:, 0:P], ml_NMd[:, b, :], ACT.Exp, bias=ml_cT[:, b, h:h + 1])
                        if b < NQ - 1:
                            last = act.activation(ml_E[:, P:n], ml_NM[:, P * (b + 1):S], ACT.Exp,
                                                  bias=ml_cT[:, b, h:h + 1])
                        last.then_inc(act_out, 1)
                        k.up(act_out)
                    k.up(dve_out)
                    k.up(pe_out, 2 * NQ)
                    act.wait_ge(dve_out, k.up(dve_out))
                    square(ml_h[:, :])
                    guess(4, 1.0 / P, var[:, :], r0[:, :])
                    act.activation(ml_E[:, :], ml_U[:, 8 + h, :], ACT.Sigmoid).then_inc(act_out, 1)
                    k.up(act_out)
                    split(yb_hi[:, h, :], 1)
                stage_end(act, "act", k, 9)
            if NSTAGES >= 10:
                begin(k, 10)
                with k.repeat(act, 2, {tile_done: 4, read_out: 4, **prep_rates(4)}) as i:
                    for u in range(4):
                        prep()
                        act.wait_ge(tile_done, k.up(tile_done))
                        b = bank_of(k.n["prep"] - AHEAD - 1)
                        copy(chunk(ds_U, 4 * i + u), ps[:, b:b + 1, :]).then_inc(read_out, 1)
                        k.up(read_out)
                for u in range(3):
                    prep()
                    act.wait_ge(tile_done, k.up(tile_done))
                    copy(ds_kvi[:, u, :], ps[:, bank_of(k.n["prep"] - AHEAD - 1), :]).then_inc(read_out, 1)
                    act.wait_ge(read_out, k.up(read_out))
                act.wait_ge(pe_out, k.up(pe_out))
                copy(ds_V[:, :, :], ps[:, 0, :].rearrange("p (b v) -> p b v", v=P)).then_inc(act_out, 1)
                k.up(act_out)
                for src in DSA_NORMED(ds_U, ds_kvi):
                    square(src[0])
                    guess(4, 1.0 / HEAD, var[:, :], r0[:, :])
                    k.up(n_done)
                for b in range(1, NQ):
                    for h in range(8):
                        act.wait_ge(pe_out, k.up(pe_out))
                        if h >= 2 or b > 1:
                            act.wait_ge(dve_out, k.up(dve_out))
                        act.activation(ds_P[:, h % 2, 0:P * (b + 1)], ps[:, 4 + h % 2, 0:P * (b + 1)], ACT.Relu)\
                            .then_inc(act_out, 1)
                        k.up(act_out)
                k.up(dve_out, 2)
                units = [(c, half, b) for c in range(4) for half in range(2) for b in range(NQ)]

                def exps(u):
                    n = P * (units[u][2] + 1)
                    act.wait_ge(m_done, k.up(m_done))
                    act.activation(ds_P[:, u % 2, 0:n], ds_P[:, u % 2, 0:n], ACT.Exp, bias=ds_st[:, u, 1:2],
                                   accum_out=ds_st[:, u, 2:3]).then_inc(e_done, 1)
                    k.up(e_done)

                exps(0)
                for u in range(32):
                    if u < 31:
                        exps(u + 1)
                    n = P * (units[u][2] + 1)
                    act.wait_ge(t_done, k.up(t_done))
                    if u >= 2:
                        act.wait_ge(o_done, k.up(o_done))
                    copy(ds_PT[:, u % 2, 0:n], ps[:, 6 + u % 2, 0:n]).then_inc(pt_done, 1)
                    k.up(pt_done)
                    if u % 8 == 7:
                        c = u // 8
                        if u == 31:
                            k.up(o_done, 2)
                            act.wait_ge(o_done, k.at(o_done))
                        else:
                            act.wait_ge(o_done, k.at(o_done, 2))
                        copy(ya_hi[:, c, :], ps[:, c % 2, :]).then_inc(split_hi, 1)
                        k.up(split_hi)
                stage_end(act, "act", k, 10)
            if NSTAGES >= 11:
                begin(k, 11)
                with k.repeat(act, 2, {tile_done: 12, gated: 4, tmp_done: 2, split_hi: 2, **prep_rates(12)}) as i:
                    for m in range(2):
                        for g in range(2):
                            for _ in range(3):
                                prep()
                            act.wait_ge(tile_done, k.up(tile_done, 3))
                            act.activation(mg_s[:, 2 * g:2 * g + 2, :], ps[:, 4 * g:4 * g + 2, :], ACT.Sigmoid)\
                                .then_inc(gated, 1)
                            k.up(gated)
                        act.wait_ge(tmp_done, k.up(tmp_done))
                        copy(m_hi[:, bass.ds(4 * i + 2 * m, 2), :], mg_t[:, :, :]).then_inc(split_hi, 1)
                        k.up(split_hi)
                stage_end(act, "act", k, 11)
            if NSTAGES >= 12:
                begin(k, 12)
                adds_to_x(8, 4)
                stage_end(act, "act", k, 12)
            if NSTAGES >= 13:
                begin(k, 13)
                ffn_up()
                stage_end(act, "act", k, 13)
            if NSTAGES >= 14:
                begin(k, 14)
                adds_to_x(24, 12)
                stage_end(act, "act", k, 14)

        @block.vector
        def _(dve):
            k = Counts()

            def link(instr):
                instr.then_inc(dve_chain, 1)
                dve.wait_ge(dve_chain, k.up(dve_chain))

            def prep():
                n = k.n.get("prep", 0)
                s = n % RING
                dve.wait_ge(hi_done, k.up(hi_done))
                dve.tensor_tensor(w_lo[:, s, :], w_raw[:, s, :], w_hi[:, s, :].bitcast(F32), ALU.subtract)\
                    .then_inc(lo_done, 1)
                k.up("prep")

            def prep_rates(tiles):
                return {"prep": tiles, hi_done: tiles}

            def newton(var_ap, r0_ap):
                dve.wait_ge(r0_done, k.up(r0_done))
                link(dve.tensor_tensor(rs[:, :], r0_ap, r0_ap, ALU.mult))
                link(dve.scalar_tensor_tensor(rs[:, :], rs[:, :], -0.5, var_ap, ALU.mult, ALU.mult))
                dve.scalar_tensor_tensor(rs[:, :], rs[:, :], 1.5, r0_ap, ALU.add, ALU.mult).then_inc(rs_done, 1)
                dve.wait_ge(rs_done, k.up(rs_done))

            def split(dst, src, hi):
                dve.wait_ge(split_hi, k.up(split_hi))
                dve.tensor_tensor(dst, src, hi.bitcast(F32), ALU.subtract).then_inc(split_lo, 1)
                k.up(split_lo)

            def norm(src, gain):
                newton(var[:, :], r0[:, :])
                for c in range(KC + 1):
                    if c < KC:
                        if c >= 2:
                            dve.wait_ge(split_lo, k.at(split_lo))
                        dve.scalar_tensor_tensor(tmp[:, c % 2, :], src[:, c, :], col(gain, c), rs[:, :], ALU.mult,
                                                 ALU.mult).then_inc(tmp_done, 1)
                        k.up(tmp_done)
                    if c:
                        split(H_lo[:, c - 1, :], tmp[:, (c - 1) % 2, :], H_hi[:, c - 1, :])

            def ple(gain):
                dve.wait_ge(act_out, k.up(act_out))
                dve.tensor_tensor(pl_lo[:, :, :], pl_raw[:, :, :], pl_hi[:, :, :].bitcast(F32), ALU.subtract)\
                    .then_inc(dve_out, 1)
                k.up(dve_out)
                k.up(read_out, 2)
                prep()
                norm(X, gain)
                prep()
                with k.repeat(dve, 2, {gated: 4, read_out: 4, dve_chain: 4, **prep_rates(4)}) as i:
                    for u in range(4):
                        prep()
                        dve.wait_ge(gated, k.up(gated))
                        m = 4 * i + u
                        v = slice(u % 2, u % 2 + 1)
                        dve.wait_ge(read_out, k.at(read_out, -1))
                        link(dve.tensor_tensor(tmp[:, v, :], sq[:, v, :], chunk(pl_P, m), ALU.mult))
                        dve.tensor_tensor(chunk(X, m), chunk(X, m), tmp[:, v, :], ALU.add).then_inc(read_out, 1)
                        k.up(read_out)

            def adds_to_x(tiles, body, parts, scale):
                n = body // parts
                with k.repeat(dve, tiles // body, {tile_done: body, **prep_rates(body)}) as i:
                    for u in range(n):
                        for _ in range(parts):
                            prep()
                        dve.wait_ge(tile_done, k.up(tile_done, parts))
                        bank = bank_of(k.n["prep"] - AHEAD - 1) if parts == 1 else u
                        x = chunk(X, n * i + u)
                        dve.scalar_tensor_tensor(x, ps[:, bank:bank + 1, :], scale, x, ALU.mult, ALU.add)\
                            .then_inc(read_out, 1)

            def ffn_up(gain):
                norm(X, gain)
                with k.repeat(dve, FF // 2, {gated: 2, split_hi: 2, split_lo: 2, tile_done: 4,
                                             **prep_rates(4)}) as i:
                    for j in range(2):
                        prep()
                        prep()
                        dve.wait_ge(gated, k.up(gated))
                        dve.wait_ge(tile_done, k.up(tile_done, 2))
                        b = bank_of(k.n["prep"] - AHEAD - 1)
                        dve.tensor_tensor(tmp[:, j, :], sq[:, j, :], ps[:, b, :], ALU.mult).then_inc(read_out, 1)
                        split(chunk(mid_lo, 2 * i + j), tmp[:, j:j + 1, :], chunk(mid_hi, 2 * i + j))

            for _ in range(4):
                dve.drain().then_inc(read_out, 1)
            dve.wait_ge(par_loaded, 16)
            dve.wait_ge(x_loaded, 16)
            for _ in range(AHEAD):
                prep()
            begin(k, 1)
            norm(X, "norm_g0")
            with k.repeat(dve, 4, {gated: 2, dve_chain: 63, **prep_rates(4)}) as i:
                for j in range(2):
                    prep()
                    prep()
                    dve.wait_ge(gated, k.up(gated))
                    dve.tensor_tensor(cv_a[:, j, :], ps[:, 2 * j, :], cv_sg[:, j, :], ALU.mult).then_inc(read_out, 1)
                link(dve.tensor_copy(flat(cv_w[:, :, :]), par[:, bass.ds(64 * i + PARAMS["taps"], 64)]))
                for t in range(CONV_W):
                    for j in range(2):
                        w = cv_w[:, j, CONV_W - 1 - t:CONV_W - t]
                        if t == 0:
                            instr = dve.tensor_scalar(cv_acc[:, j, :], cv_a[:, j, :], w, cv_w[:, j, CONV_W:CONV_W + 1],
                                                      ALU.mult, ALU.add)
                        else:
                            dve.wait_ge(dve_chain, k.at(dve_chain, -1))
                            o = cv_acc[:, j, t:S] if t < CONV_W - 1 else cv_Y[:, bass.ds(2 * i + j, 1), t:S]
                            acc = cv_acc[:, j, t:S] if t < CONV_W - 1 else cv_acc[:, j:j + 1, t:S]
                            a = cv_a[:, j, 0:S - t] if t < CONV_W - 1 else cv_a[:, j:j + 1, 0:S - t]
                            instr = dve.scalar_tensor_tensor(o, a, w, acc, ALU.mult, ALU.add)
                        instr.then_inc(dve_chain, 1)
                        k.up(dve_chain)
                dve.wait_ge(dve_chain, k.at(dve_chain))
                for j in range(2):
                    dve.tensor_copy(cv_Y[:, bass.ds(2 * i + j, 1), 0:CONV_W - 1], cv_acc[:, j:j + 1, 0:CONV_W - 1])
            with k.repeat(dve, 2, {**prep_rates(4)}):
                for u in range(4):
                    prep()
            stage_end(dve, "dve", k, 1)
            if NSTAGES >= 2:
                begin(k, 2)
                dve.wait_ge(pe_out, k.up(pe_out))
                for c in range(KC):
                    dve.scalar_tensor_tensor(cv_Y[:, c, :], ps[:, 5, :], -1.0 / D, cv_Y[:, c, :], ALU.mult, ALU.add)\
                        .then_inc(n_done, 1)
                    k.up(n_done)
                newton(var[:, :], r0[:, :])
                for c in range(KC + 1):
                    if c < KC:
                        dve.scalar_tensor_tensor(tmp[:, c % 2, :], cv_Y[:, c, :], col("ln_g", c), rs[:, :], ALU.mult,
                                                 ALU.mult).then_inc(tmp_done, 1)
                        dve.wait_ge(act_out, k.up(act_out))
                        dve.tensor_tensor(cv_Y[:, c, :], sq[:, c % 2, :], cv_G[:, c, :], ALU.mult).then_inc(tmp_done, 1)
                        k.up(tmp_done, 2)
                    if c:
                        split(H_lo[:, c - 1, :], cv_Y[:, c - 1, :], H_hi[:, c - 1, :])
                adds_to_x(8, 4, 1, 1.0)
                stage_end(dve, "dve", k, 2)
            if NSTAGES >= 3:
                begin(k, 3)
                ple("ple_g0")
                stage_end(dve, "dve", k, 3)
            if NSTAGES >= 4:
                begin(k, 4)
                dve.wait_ge(pos_loaded, 16)
                link(dve.tensor_copy(at_vT[:, 0, :], at_SG[:, :].bitcast(I32)))
                ang = at_vT[:, 1, :]
                link(dve.tensor_scalar(ang, at_vT[:, 0, :], col("inv_freq"), None, ALU.mult))
                for dst, turn, shift in ((at_C, 0.0, 0.0), (at_SG, 0.25, float(np.pi / 2))):
                    n = at_vT[:, 2, :]
                    link(dve.tensor_scalar(n, ang, 1.0 / (2 * np.pi), turn, ALU.mult, ALU.add))
                    link(dve.tensor_scalar(n, n, ROUND, None, ALU.add))
                    link(dve.tensor_scalar(n, n, ROUND, None, ALU.subtract))
                    link(dve.scalar_tensor_tensor(dst[:, :], n, -TURN[0], ang, ALU.mult, ALU.add))
                    link(dve.tensor_scalar(dst[:, :], dst[:, :], shift, None, ALU.add))
                    for part in TURN[1:]:
                        link(dve.scalar_tensor_tensor(dst[:, :], n, -part, dst[:, :], ALU.mult, ALU.add))
                    link(dve.tensor_scalar(dst[:, :], dst[:, :], PI, -PI, ALU.min, ALU.max))
                for j, gain in enumerate(("q_norm", "k_norm")):
                    dve.tensor_scalar(at_G[:, 2 * j, :], ident, col(gain), None, ALU.mult)
                    dve.tensor_scalar(at_G[:, 2 * j + 1, :], const("rot"), col(gain), None, ALU.mult)
                dve.drain().then_inc(dve_out, 1)
                k.up(dve_out)
                k.up(act_out)
                norm(X, "norm_g1")
                stage_end(dve, "dve", k)
                rates = {act_out: 2, pe_out: 2, dve_chain: 12 * 2 + 16 * 2, r0_done: 12, rs_done: 12, n_done: 12,
                         **{s: 16 for s in (m_done, e_done, p_done, s_done)}, t_done: 16, o_done: 16, rot_done: 12,
                         tmp_done: 2, split_hi: 2, split_lo: 2, **{e: 2 for e in ended.values()}, **prep_rates(20)}
                with k.repeat(dve, 2, rates) as i:
                    for cc in range(2):
                        for j in range(10):
                            prep()
                        k.up(act_out)
                        k.up(pe_out)
                        for j in range(6):
                            newton(at_var[:, j % 2, :], at_r0[:, j % 2, :])
                            dve.wait_ge(rot_done, k.up(rot_done))
                            dve.tensor_tensor(at_raw[:, RAW[j], :], ps[:, 6 + j % 2, :], rs[:, :], ALU.mult)\
                                .then_inc(n_done, 1)
                            dve.wait_ge(n_done, k.up(n_done))

                        def masked(u):
                            dve.wait_ge(s_done, k.up(s_done))
                            if u >= 2:
                                dve.wait_ge(t_done, k.up(t_done))
                            b = 4 + 2 * (u % 2)
                            dve.memset(at_st[:, u, 3:4], 0.0)
                            link(dve.tensor_tensor_reduce(
                                out=at_Sm[:, u % 2, :], in0=flat(ps[:, b:b + 2, :])[:, 0:768], in1=at_mask[:, u % 4, :],
                                scale=HEAD ** -0.5, scalar=TAKEN, op0=ALU.add, op1=ALU.max,
                                accum_out=at_st[:, u, 0:1]))
                            dve.tensor_scalar(at_st[:, u, 1:2], at_st[:, u, 0:1], -1.0, None, ALU.mult)\
                                .then_inc(m_done, 1)
                            k.up(m_done)

                        if cc == 0:
                            dve.wait_ge(mask_loaded, 16)
                        masked(0)
                        for u in range(8):
                            if u < 7:
                                masked(u + 1)
                            dve.wait_ge(e_done, k.up(e_done))
                            link(dve.reciprocal(at_st[:, u, 3:4], at_st[:, u, 2:3]))
                            dve.tensor_scalar(at_Sm[:, u % 2, :], at_Sm[:, u % 2, :], at_st[:, u, 3:4], None, ALU.mult)\
                                .then_inc(p_done, 1)
                            k.up(p_done)
                        k.up(t_done, 2)
                        dve.wait_ge(o_done, k.up(o_done, 8))
                        dve.tensor_tensor(tmp[:, cc, :].rearrange("p (l r) -> p r l", r=4),
                                          ps[:, 2 + cc, :].rearrange("p (r l) -> p r l", r=4),
                                          at_SG[:, :].rearrange("p (l r) -> p r l", r=4), ALU.mult).then_inc(tmp_done, 1)
                        k.up(tmp_done)
                        split(chunk(at_Yl, 2 * i + cc), tmp[:, cc:cc + 1, :], chunk(at_Yh, 2 * i + cc))
                        stage_end(dve, "dve", k)
                stage_end(dve, "dve", k, 4)
            if NSTAGES >= 5:
                begin(k, 5)
                for m in range(4):
                    prep()
                    dve.wait_ge(tile_done, k.up(tile_done))
                    b = 2 * (m % 2)
                    dve.tensor_tensor(X[:, 2 * m:2 * m + 2, :], ps[:, b:b + 2, :], X[:, 2 * m:2 * m + 2, :], ALU.add)\
                        .then_inc(read_out, 1)
                stage_end(dve, "dve", k, 5)
            if NSTAGES >= 6:
                begin(k, 6)
                ple("ple_g1")
                stage_end(dve, "dve", k, 6)
            if NSTAGES >= 7:
                begin(k, 7)
                ffn_up("ffn1")
                stage_end(dve, "dve", k, 7)
            if NSTAGES >= 8:
                begin(k, 8)
                adds_to_x(24, 12, 3, 0.5)
                stage_end(dve, "dve", k, 8)
            if NSTAGES >= 9:
                begin(k, 9)
                norm(X, "mix")
                with k.repeat(dve, 3, {**prep_rates(4)}):
                    for u in range(4):
                        prep()
                prep()
                k.up(read_out, 13)
                k.up(pe_out)
                k.up(act_out)
                dve.wait_ge(read_out, k.at(read_out))
                dve.tensor_copy(ml_g[:, 0, :], ml_sm[32:36, :])
                link(dve.tensor_copy(ml_g[:, 1, :], ml_sm[64:68, :]))
                dve.tensor_scalar(ml_g[:, 0, :], ml_g[:, 0, :], par[0:4, PARAMS["b_i"]:PARAMS["b_i"] + 1], None, ALU.add)
                dve.tensor_scalar(ml_g[:, 1, :], ml_g[:, 1, :], par[0:4, PARAMS["b_f"]:PARAMS["b_f"] + 1], None, ALU.add)\
                    .then_inc(dve_out, 1)
                dve.wait_ge(dve_out, k.up(dve_out))
                dve.wait_ge(act_out, k.up(act_out))
                link(dve.scalar_tensor_tensor(ml_g[:, 1, :], ml_g[:, 1, :], 0.0, ml_m[:, 0, :], ALU.min, ALU.subtract))
                link(dve.memset(ml_g[:, 3, :], 1.0))
                link(dve.tensor_tensor_scan(ml_g[:, 2, :], ml_g[:, 3, :], ml_g[:, 1, :], 0.0, ALU.mult, ALU.add))
                link(dve.tensor_tensor(ml_c[:, :], ml_g[:, 0, :], ml_g[:, 2, :], ALU.subtract))
                link(dve.tensor_tensor_scan(ml_g[:, 3, :], ml_c[:, :], ml_c[:, :], 0.0, ALU.max, ALU.max))
                link(dve.tensor_scalar(ml_m[:, 0, :], ml_g[:, 3, :], -1.0, None, ALU.mult))
                dve.tensor_tensor(ml_m[:, 1, :], ml_m[:, 0, :], ml_g[:, 2, :], ALU.subtract).then_inc(dve_out, 1)
                k.up(dve_out)
                k.up(pe_out)
                k.up(act_out)
                for h in range(MH):
                    u = ml_U[:, h, :]
                    if h:
                        dve.wait_ge(split_lo, k.at(split_lo))
                    link(dve.tensor_scalar(ml_h[:, :], u, col("conv2", 4 * h + 3), col("conv2_b", h), ALU.mult, ALU.add))
                    for t in (1, 2, 3):
                        instr = dve.scalar_tensor_tensor(ml_h[:, t:S], ml_U[:, h, 0:S - t], col("conv2", 4 * h + 3 - t),
                                                         ml_h[:, t:S], ALU.mult, ALU.add)
                        if t < 3:
                            link(instr)
                    instr.then_inc(dve_out, 1)
                    k.up(dve_out)
                    k.up(act_out)
                    k.up(pe_out)
                    dve.wait_ge(act_out, k.up(act_out))
                    for b in range(NQ):
                        instr = dve.tensor_tensor(ml_NMd[:, b, :], ml_NM[:, b * P:(b + 1) * P], const("diag_causal"),
                                                  ALU.add)
                    instr.then_inc(dve_out, 1)
                    k.up(dve_out)
                    for b in range(NQ):
                        n = S - P * b
                        dve.wait_ge(act_out, k.up(act_out))
                        dve.wait_ge(pe_out, k.up(pe_out, 1 if b == 0 else 2))
                        dve.scalar_tensor_tensor(ml_W[:, 0:n], ps[:, 4 + b % 2, 0:n], HEAD ** -0.5, ml_E[:, 0:n],
                                                 ALU.mult, ALU.mult).then_inc(dve_out, 1)
                        k.up(dve_out)
                    dve.wait_ge(pe_out, k.up(pe_out))
                    link(dve.tensor_scalar(ml_W[:, :], ps[:, 3, :], -1.0, None, ALU.mult))
                    link(dve.tensor_tensor(ml_W[:, :], ps[:, 3, :], ml_W[:, :], ALU.max))
                    link(dve.tensor_tensor(ml_W[:, :], ml_W[:, :], ml_EB[:, :], ALU.max))
                    link(dve.reciprocal(ml_W[:, :], ml_W[:, :]))
                    dve.tensor_tensor(ml_h[:, :], ps[:, 2, :], ml_W[:, :], ALU.mult).then_inc(dve_out, 1)
                    k.up(dve_out)
                    newton(var[:, :], r0[:, :])
                    link(dve.scalar_tensor_tensor(tmp[:, 0, :], ml_h[:, :], col("m_head", h), rs[:, :], ALU.mult,
                                                  ALU.mult))
                    dve.wait_ge(act_out, k.up(act_out))
                    dve.tensor_tensor(tmp[:, 1, :], tmp[:, 0, :], ml_E[:, :], ALU.mult).then_inc(tmp_done, 1)
                    k.up(tmp_done)
                    split(yb_lo[:, h, :], tmp[:, 1, :], yb_hi[:, h, :])
                stage_end(dve, "dve", k, 9)
            if NSTAGES >= 10:
                begin(k, 10)
                with k.repeat(dve, 2, {**prep_rates(4)}):
                    for _ in range(4):
                        prep()
                for _ in range(3):
                    prep()
                k.up(pe_out)
                k.up(act_out)
                k.up(read_out, 11)
                dve.wait_ge(read_out, k.at(read_out))
                for src, gain in DSA_NORMED(ds_U, ds_kvi):
                    newton(var[:, :], r0[:, :])
                    dve.scalar_tensor_tensor(src, src, col(gain), rs[:, :], ALU.mult, ALU.mult).then_inc(n_done, 1)
                    dve.wait_ge(n_done, k.up(n_done))
                for b in range(1, NQ):
                    n = P * (b + 1)
                    acc = ds_acc[:, 0:n]
                    for h in range(8):
                        dve.wait_ge(act_out, k.up(act_out))
                        if h == 0:
                            instr = dve.tensor_scalar(acc, ds_P[:, 0, 0:n], IW[:, b, 0:1], None, ALU.mult)
                        else:
                            instr = dve.scalar_tensor_tensor(acc, ds_P[:, h % 2, 0:n], IW[:, b, h:h + 1], acc,
                                                             ALU.mult, ALU.add)
                        instr.then_inc(dve_out, 1)
                        dve.wait_ge(dve_out, k.up(dve_out))
                    link(dve.tensor_tensor(ds_acc[:, b * P:n], ds_acc[:, b * P:n], const("diag_block"), ALU.add))
                    for _ in range(TOPK // 8):
                        link(dve.max(ds_mx[:, :], acc))
                        link(dve.match_replace(acc, ds_mx[:, :], acc, TAKEN))
                    link(dve.tensor_scalar(acc, acc, TAKEN, -NEG, ALU.is_equal, ALU.mult))
                    link(dve.tensor_scalar(ds_bias[:, b, 0:n], acc, NEG, None, ALU.add))
                k.up(pe_out, 24)
                units = [(c, half, b) for c in range(4) for half in range(2) for b in range(NQ)]

                def masked(u):
                    b = units[u][2]
                    n = P * (b + 1)
                    if u >= 2:
                        dve.wait_ge(t_done, k.up(t_done))
                    dve.wait_ge(s_done, k.up(s_done))
                    bias = const("diag_block") if b == 0 else ds_bias[:, b, 0:n]
                    link(dve.tensor_tensor_reduce(out=ds_P[:, u % 2, 0:n], in0=ps[:, 4 + u % 2, 0:n], in1=bias,
                                                  scale=HEAD ** -0.5, scalar=TAKEN, op0=ALU.add, op1=ALU.max,
                                                  accum_out=ds_st[:, u, 0:1]))
                    dve.tensor_scalar(ds_st[:, u, 1:2], ds_st[:, u, 0:1], -1.0, None, ALU.mult).then_inc(m_done, 1)
                    k.up(m_done)

                masked(0)
                for u in range(32):
                    if u < 31:
                        masked(u + 1)
                    n = P * (units[u][2] + 1)
                    dve.wait_ge(e_done, k.up(e_done))
                    link(dve.reciprocal(ds_st[:, u, 3:4], ds_st[:, u, 2:3]))
                    dve.tensor_scalar(ds_P[:, u % 2, 0:n], ds_P[:, u % 2, 0:n], ds_st[:, u, 3:4], None, ALU.mult)\
                        .then_inc(p_done, 1)
                    k.up(p_done)
                    if u % 8 == 7:
                        c = u // 8
                        dve.wait_ge(split_hi, k.up(split_hi))
                        dve.tensor_tensor(ya_lo[:, c, :], ps[:, c % 2, :], ya_hi[:, c, :].bitcast(F32), ALU.subtract)\
                            .then_inc(split_lo, 1)
                        k.up(split_lo)
                k.up(t_done, 2)
                k.up(o_done, 32)
                stage_end(dve, "dve", k, 10)
            if NSTAGES >= 11:
                begin(k, 11)
                with k.repeat(dve, 2, {gated: 4, read_out: 4, tmp_done: 2, split_hi: 2, split_lo: 2,
                                       **prep_rates(12)}) as i:
                    for m in range(2):
                        for g in range(2):
                            for _ in range(3):
                                prep()
                            dve.wait_ge(gated, k.up(gated))
                            if g == 0:
                                dve.wait_ge(split_lo, k.at(split_lo))
                            out_t = mg_t if g == 0 else mg_s[:, 2:4, :]
                            dve.tensor_tensor(out_t[:, :, :], mg_s[:, 2 * g:2 * g + 2, :],
                                              ps[:, 4 * g + 2:4 * g + 4, :], ALU.mult).then_inc(read_out, 1)
                            k.up(read_out)
                        dve.wait_ge(read_out, k.at(read_out))
                        dve.tensor_tensor(mg_t[:, :, :], mg_t[:, :, :], mg_s[:, 2:4, :], ALU.add).then_inc(tmp_done, 1)
                        k.up(tmp_done)
                        at = bass.ds(4 * i + 2 * m, 2)
                        split(m_lo[:, at, :], mg_t[:, :, :], m_hi[:, at, :])
                stage_end(dve, "dve", k, 11)
            if NSTAGES >= 12:
                begin(k, 12)
                adds_to_x(8, 4, 1, 1.0)
                stage_end(dve, "dve", k, 12)
            if NSTAGES >= 13:
                begin(k, 13)
                ffn_up("ffn2")
                stage_end(dve, "dve", k, 13)
            if NSTAGES >= 14:
                begin(k, 14)
                adds_to_x(24, 12, 3, 0.5)
                stage_end(dve, "dve", k, 14)

        @block.tensor
        def _(pe):
            k = Counts()

            def tile(groups):
                s = k.n.get("tile", 0) % RING
                k.up("tile")
                pe.wait_ge(lo_done, k.up(lo_done))
                for bank, first, last, blocks in groups:
                    for n, (b, x_hi, x_lo) in enumerate(blocks):
                        wh = w_hi[:, s, b * P:(b + 1) * P]
                        wl = w_lo[:, s, b * P:(b + 1) * P]
                        for q, (w, x) in enumerate(((wh, x_hi), (wh, x_lo), (wl, x_hi))):
                            mm = pe.matmul(ps[:, bank, :], w, x, start=first and n == 0 and q == 0,
                                           stop=last and n == len(blocks) - 1 and q == 2)
                mm.then_inc(tile_done, 1)

            def blocks(hi, lo, n=KC, at=0, first=0):
                return [(first + b, hi[:, at + b, :], lo[:, at + b, :]) for b in range(n)]

            def single(hi, lo):
                pe.wait_ge(read_out, k.at(read_out, -3))
                tile([(bank_of(k.n["tile"]), True, True, blocks(hi, lo))])
                k.up(read_out)

            def pair(hi, lo):
                pe.wait_ge(read_out, k.at(read_out, -1))
                for _ in range(2):
                    tile([(bank_of(k.n["tile"]), True, True, blocks(hi, lo))])
                k.up(read_out)

            def sum_squares(c, n, bank=4, lhsT=None):
                pe.wait_ge(sq_done, k.up(sq_done))
                pe.matmul(ps[:, bank, :], ones if lhsT is None else lhsT, sq[:, (k.n[sq_done] - 1) % 2, :],
                          start=c == 0, stop=c == n - 1).then_inc(sq_used, 1)
                k.up(sq_used)

            def norm(apply=True):
                if k.n.get(r0_done, 0):
                    pe.wait_ge(r0_done, k.at(r0_done))
                for c in range(KC):
                    sum_squares(c, KC)
                k.up(r0_done)
                if apply:
                    k.up(split_lo, KC)

            def ready():
                pe.wait_ge(split_lo, k.at(split_lo))

            def ple():
                pe.wait_ge(dve_out, k.up(dve_out))
                k.up(act_out)
                for half in range(2):
                    pe.wait_ge(read_out, k.at(read_out))
                    tile([(m, True, True, blocks(pl_hi, pl_lo, n=2, first=2 * m)) for m in range(4)])
                    k.up(read_out)
                    if half == 0:
                        norm()
                ready()
                pe.wait_ge(read_out, k.at(read_out))
                with k.repeat(pe, 2, {"tile": 4, lo_done: 4, read_out: 4}):
                    for _ in range(4):
                        single(H_hi, H_lo)

            def down():
                with k.repeat(pe, 2, {"tile": 12, lo_done: 12, read_out: 4}):
                    for m in range(4):
                        pe.wait_ge(read_out, k.at(read_out, -3))
                        for part in range(3):
                            n = min(KC, FF - KC * part)
                            tile([(m, part == 0, part == 2, blocks(mid_hi, mid_lo, n=n, at=KC * part))])
                        k.up(read_out)

            def up():
                norm()
                ready()
                with k.repeat(pe, FF // 2, {"tile": 4, lo_done: 4, read_out: 2}):
                    for _ in range(2):
                        pair(H_hi, H_lo)
                k.up(split_lo, FF)

            begin(k, 1)
            pe.wait_ge(con_loaded, 16)
            norm()
            ready()
            with k.repeat(pe, 4, {"tile": 4, lo_done: 4, read_out: 2}):
                for _ in range(2):
                    pair(H_hi, H_lo)
            pe.wait_ge(read_out, k.at(read_out))
            with k.repeat(pe, 2, {"tile": 4, lo_done: 4, read_out: 4}):
                for _ in range(4):
                    single(H_hi, H_lo)
            stage_end(pe, "pe", k, 1)
            if NSTAGES >= 2:
                begin(k, 2)
                for c in range(KC):
                    mm = pe.matmul(ps[:, 5, :], ones, cv_Y[:, c, :], start=c == 0, stop=c == KC - 1)
                mm.then_inc(pe_out, 1)
                k.up(pe_out)
                k.up(n_done, KC)
                norm()
                k.up(act_out, KC)
                ready()
                with k.repeat(pe, 2, {"tile": 4, lo_done: 4, read_out: 4}):
                    for _ in range(4):
                        single(H_hi, H_lo)
                stage_end(pe, "pe", k, 2)
            if NSTAGES >= 3:
                begin(k, 3)
                ple()
                stage_end(pe, "pe", k, 3)
            if NSTAGES >= 4:
                begin(k, 4)
                norm()
                ready()
                k.up(dve_out)
                k.up(act_out)
                stage_end(pe, "pe", k)
                rates = {"tile": 20, lo_done: 20, read_out: 20, pe_out: 2, act_out: 2, sq_done: 12, sq_used: 12,
                         r0_done: 12, n_done: 12, pool_out: 24, rot_done: 12,
                         **{s: 16 for s in (s_done, m_done, p_done, t_done, pt_done, o_done)}, split_lo: 2,
                         **{e: 2 for e in ended.values()}}
                with k.repeat(pe, 2, rates):
                    for cc in range(2):
                        for _ in range(10):
                            single(H_hi, H_lo)
                        pe.wait_ge(read_out, k.at(read_out))
                        for g in range(GROUPS):
                            for b in range(NQ):
                                v = at_vT[:, g, b * P:(b + 1) * P] if g == 0 else at_vT[:, g, b:S:4]
                                mm = pe.transpose(ps[:, g, b * P:(b + 1) * P], v, ident)
                        mm.then_inc(pe_out, 1)
                        k.up(pe_out)

                        def sums(j):
                            if j >= 2:
                                pe.wait_ge(r0_done, k.up(r0_done))
                            sum_squares(0, 1, 4 + j % 2, head_ones)

                        sums(0)
                        for j in range(6):
                            if j < 5:
                                sums(j + 1)
                            pe.wait_ge(pool_out, k.up(pool_out, 2))
                            if j >= 2:
                                pe.wait_ge(n_done, k.up(n_done))
                            for n in range(2):
                                mm = pe.matmul(ps[:, 6 + j % 2, :], at_G[:, 2 * (j % 2) + n, :],
                                               at_ab[:, 2 * (j % 2) + n, :], start=n == 0, stop=n == 1)
                            mm.then_inc(rot_done, 1)
                            k.up(rot_done)
                        k.up(r0_done, 2)
                        pe.wait_ge(n_done, k.up(n_done, 2))
                        pe.wait_ge(act_out, k.up(act_out))

                        def scores(u):
                            rows, r = slice(HEAD * (u // 4), HEAD * (u // 4) + HEAD), u % 4
                            if u >= 2:
                                pe.wait_ge(m_done, k.up(m_done))
                            b = 4 + 2 * (u % 2)
                            pe.matmul(ps[:, b, :], at_raw[rows, 0, r:S:4], at_raw[rows, 1, :], start=True, stop=True)
                            for g in (1, 2):
                                mm = pe.matmul(ps[:, b + 1, (g - 1) * P:g * P], at_raw[rows, 2 * g, r:S:4],
                                               at_raw[rows, 2 * g + 1, r:S:4], start=True, stop=True)
                            mm.then_inc(s_done, 1)
                            k.up(s_done)

                        scores(0)
                        scores(1)
                        for u in range(8):
                            rows, r = slice(HEAD * (u // 4), HEAD * (u // 4) + HEAD), u % 4
                            pe.wait_ge(p_done, k.up(p_done))
                            if u:
                                pe.wait_ge(pt_done, k.at(pt_done))
                            for b in range(6):
                                mm = pe.transpose(ps[:, b // 4, (b % 4) * P:(b % 4 + 1) * P],
                                                  at_Sm[:, u % 2, b * P:(b + 1) * P], ident)
                            mm.then_inc(t_done, 1)
                            k.up(t_done)
                            if u < 6:
                                scores(u + 2)
                            pe.wait_ge(pt_done, k.up(pt_done))
                            for b in range(6):
                                g, v = (0, b) if b < 4 else (b - 3, r)
                                mm = pe.matmul(ps[rows, 2 + cc, r * P:(r + 1) * P],
                                               at_V[:, g, v * P + rows.start:v * P + rows.stop],
                                               at_PT[:, b * P:(b + 1) * P], start=b == 0, stop=b == 5)
                            mm.then_inc(o_done, 1)
                            k.up(o_done)
                        k.up(m_done, 2)
                        k.up(split_lo)
                        stage_end(pe, "pe", k)
                stage_end(pe, "pe", k, 4)
            if NSTAGES >= 5:
                begin(k, 5)
                for m in range(4):
                    pe.wait_ge(read_out, k.at(read_out, -1))
                    tile([(2 * (m % 2) + n, True, True, blocks(at_Yh, at_Yl, n=4, first=4 * n)) for n in range(2)])
                    k.up(read_out)
                stage_end(pe, "pe", k, 5)
            if NSTAGES >= 6:
                begin(k, 6)
                ple()
                stage_end(pe, "pe", k, 6)
            if NSTAGES >= 7:
                begin(k, 7)
                up()
                stage_end(pe, "pe", k, 7)
            if NSTAGES >= 8:
                begin(k, 8)
                down()
                stage_end(pe, "pe", k, 8)
            if NSTAGES >= 9:
                begin(k, 9)
                norm()
                ready()
                with k.repeat(pe, 3, {"tile": 4, lo_done: 4, read_out: 4}):
                    for _ in range(4):
                        single(H_hi, H_lo)
                single(H_hi, H_lo)
                pe.wait_ge(read_out, k.at(read_out))
                for b in range(NQ):
                    mm = pe.transpose(ps[:, 4, b * P:(b + 1) * P], ml_sm[:, b * P:(b + 1) * P], ident)
                mm.then_inc(pe_out, 1)
                k.up(pe_out)
                k.up(dve_out)
                k.up(act_out, 2)
                pe.wait_ge(dve_out, k.up(dve_out))
                for b in range(NQ):
                    mm = pe.transpose(ps[:, 5, 4 * b:4 * b + 4], ml_c[:, b * P:(b + 1) * P], ident[0:4, 0:4])
                mm.then_inc(pe_out, 1)
                k.up(pe_out)
                pe.wait_ge(act_out, k.up(act_out))
                for h in range(MH):
                    k.up(dve_out)
                    pe.wait_ge(act_out, k.up(act_out))
                    pe.matmul(ps[0:HEAD, 4, :], col("w_mq", HEAD * h, HEAD), ml_xc[:, :], start=True, stop=True)
                    pe.matmul(ps[0:HEAD, 5, :], col("w_mk", HEAD * h, HEAD), ml_xc[:, :], start=True, stop=True)
                    for n in range(2):
                        pe.matmul(ps[:, 6 + n, :], con[0:4, CONSTS["pick"] + P * h:CONSTS["pick"] + P * (h + 1)],
                                  ml_m[:, n, :], start=True, stop=True)
                    for b in range(NQ):
                        mm = pe.transpose(ps[:, 0, b * P:(b + 1) * P], ml_U[:, 4 + h, b * P:(b + 1) * P], ident)
                    mm.then_inc(pe_out, 1)
                    k.up(pe_out)
                    pe.wait_ge(act_out, k.up(act_out))
                    k.up(dve_out)

                    def scores(b):
                        n = S - P * b
                        pe.matmul(ps[:, 4 + b % 2, 0:n], ml_k[:, b * P:(b + 1) * P], ml_q[:, b * P:S],
                                  start=True, stop=True).then_inc(pe_out, 1)
                        k.up(pe_out)

                    scores(0)
                    for b in range(NQ):
                        if b < NQ - 1:
                            scores(b + 1)
                        pe.wait_ge(dve_out, k.up(dve_out))
                        n = S - P * b
                        pe.matmul(ps[:, 2, P * b:S], ml_V[:, b, :], ml_W[:, 0:n], start=b == 0, stop=b == NQ - 1,
                                  skip_group_check=True)
                        pe.matmul(ps[:, 3, P * b:S], ones, ml_W[:, 0:n], start=b == 0, stop=b == NQ - 1,
                                  skip_group_check=True).then_inc(pe_out, 1)
                        k.up(pe_out)
                    k.up(act_out, NQ)
                    k.up(dve_out)
                    if h or True:
                        pe.wait_ge(r0_done, k.at(r0_done))
                    sum_squares(0, 1)
                    k.up(r0_done)
                    k.up(act_out)
                    k.up(split_lo)
                    pe.wait_ge(split_lo, k.at(split_lo))
                stage_end(pe, "pe", k, 9)
            if NSTAGES >= 10:
                begin(k, 10)
                with k.repeat(pe, 2, {"tile": 4, lo_done: 4, read_out: 4}):
                    for _ in range(4):
                        single(H_hi, H_lo)
                for _ in range(3):
                    single(H_hi, H_lo)
                pe.wait_ge(read_out, k.at(read_out))
                for b in range(NQ):
                    mm = pe.transpose(ps[:, 0, b * P:(b + 1) * P], ds_kvi[:, 1, b * P:(b + 1) * P], ident)
                mm.then_inc(pe_out, 1)
                k.up(pe_out)
                for src in DSA_NORMED(ds_U, ds_kvi):
                    pe.wait_ge(r0_done, k.at(r0_done))
                    sum_squares(0, 1, 4, head_ones)
                    k.up(r0_done)
                pe.wait_ge(n_done, k.up(n_done, 6))
                pe.wait_ge(act_out, k.up(act_out))
                for b in range(1, NQ):
                    for h in range(8):
                        if h >= 2 or b > 1:
                            pe.wait_ge(act_out, k.up(act_out))
                        rows = slice(HEAD * (h % 2), HEAD * (h % 2) + HEAD)
                        pe.matmul(ps[:, 4 + h % 2, 0:P * (b + 1)], ds_U[rows, 4 + h // 2, b * P:(b + 1) * P],
                                  ds_kvi[rows, 2, 0:P * (b + 1)], start=True, stop=True).then_inc(pe_out, 1)
                        k.up(pe_out)
                pe.wait_ge(act_out, k.up(act_out, 2))
                k.up(dve_out, 24)
                units = [(c, half, b) for c in range(4) for half in range(2) for b in range(NQ)]

                def scores(u):
                    c, half, b = units[u]
                    rows = slice(HEAD * half, HEAD * half + HEAD)
                    if u >= 2:
                        pe.wait_ge(m_done, k.up(m_done))
                    pe.matmul(ps[:, 4 + u % 2, 0:P * (b + 1)], ds_U[rows, c, b * P:(b + 1) * P],
                              ds_kvi[rows, 0, 0:P * (b + 1)], start=True, stop=True).then_inc(s_done, 1)
                    k.up(s_done)

                scores(0)
                scores(1)
                for u in range(32):
                    c, half, b = units[u]
                    rows = slice(HEAD * half, HEAD * half + HEAD)
                    pe.wait_ge(p_done, k.up(p_done))
                    if u >= 2:
                        pe.wait_ge(pt_done, k.at(pt_done, -1))
                    for kb in range(b + 1):
                        mm = pe.transpose(ps[:, 6 + u % 2, kb * P:(kb + 1) * P], ds_P[:, u % 2, kb * P:(kb + 1) * P],
                                          ident)
                    mm.then_inc(t_done, 1)
                    k.up(t_done)
                    if u < 30:
                        scores(u + 2)
                    pe.wait_ge(pt_done, k.up(pt_done))
                    if u % 8 == 0 and c >= 2:
                        pe.wait_ge(split_lo, k.at(split_lo, c - 1))
                    for kb in range(b + 1):
                        mm = pe.matmul(ps[rows, c % 2, b * P:(b + 1) * P], ds_V[:, kb, rows],
                                       ds_PT[:, u % 2, kb * P:(kb + 1) * P], start=kb == 0, stop=kb == b)
                    mm.then_inc(o_done, 1)
                    k.up(o_done)
                k.up(m_done, 2)
                k.up(split_lo, 4)
                stage_end(pe, "pe", k, 10)
            if NSTAGES >= 11:
                begin(k, 11)
                with k.repeat(pe, 2, {"tile": 12, lo_done: 12, read_out: 4}):
                    for m in range(2):
                        for g, (y_hi, y_lo) in enumerate(((ya_hi, ya_lo), (yb_hi, yb_lo))):
                            pe.wait_ge(read_out, k.at(read_out, -1))
                            for n in range(2):
                                tile([(4 * g + n, True, True, blocks(H_hi, H_lo))])
                            tile([(4 * g + 2 + n, True, True, blocks(y_hi, y_lo, n=4, first=4 * n))
                                  for n in range(2)])
                            k.up(read_out)
                k.up(split_lo, 4)
                stage_end(pe, "pe", k, 11)
            if NSTAGES >= 12:
                begin(k, 12)
                with k.repeat(pe, 2, {"tile": 4, lo_done: 4, read_out: 4}):
                    for _ in range(4):
                        single(m_hi, m_lo)
                stage_end(pe, "pe", k, 12)
            if NSTAGES >= 13:
                begin(k, 13)
                up()
                stage_end(pe, "pe", k, 13)
            if NSTAGES >= 14:
                begin(k, 14)
                down()
                stage_end(pe, "pe", k, 14)


def _tiles(w):
    k, m = w.shape
    return w.reshape(k // P, P, m // P, P).transpose(2, 1, 0, 3)


def _cols(v):
    return np.asarray(v).reshape(-1, P).T


def kernel(x, p, positions, norm_g, conv_w_in, conv_dw, conv_dw_b, conv_ln_g, conv_ln_b, conv_w_out, attn_w_in,
           attn_q_norm, attn_k_norm, attn_w_out, ple_w_proj, ple_norm_g, ple_w_gate, ffn1_norm_2, ffn1_w_gate_2,
           ffn1_w_up_2, ffn1_w_down_2, mix_norm_2, w_in_2, q_norm_2, k_norm_2, idx_k_norm_2, conv_w_2, conv_b_2,
           w_mq_2, w_mk_2, b_i_2, b_f_2, m_head_norm_2, w_proj_a_2, w_proj_b_2, w_out_2, ffn2_norm_2,
           ffn2_w_gate_2, ffn2_w_up_2, ffn2_w_down_2):
    from concourse import bacc
    from concourse.bass_utils import run_bass_kernel_spmd

    arrays = _arrays(x, p, positions, norm_g, conv_w_in, conv_dw, conv_dw_b, conv_ln_g, conv_ln_b, conv_w_out,
                     attn_w_in, attn_q_norm, attn_k_norm, attn_w_out, ple_w_proj, ple_norm_g, ple_w_gate,
                     ffn1_norm_2, ffn1_w_gate_2, ffn1_w_up_2, ffn1_w_down_2, mix_norm_2, w_in_2, q_norm_2,
                     k_norm_2, idx_k_norm_2, conv_w_2, conv_b_2, w_mq_2, w_mk_2, b_i_2, b_f_2, m_head_norm_2,
                     w_proj_a_2, w_proj_b_2, w_out_2, ffn2_norm_2, ffn2_w_gate_2, ffn2_w_up_2, ffn2_w_down_2)
    nc = bacc.Bacc("TRN2", target_bir_lowering=False, num_devices=1)
    args = [nc.dram_tensor(n, a.shape, mybir.dt.from_np(a.dtype), kind="ExternalInput").ap()
            for n, a in arrays.items()]
    out = nc.dram_tensor("out", (P, KC, S), F32, kind="ExternalOutput").ap()
    build(nc, *args, out)
    got = run_bass_kernel_spmd(nc, [arrays], core_ids=[0]).results[0]["out"]
    return np.ascontiguousarray(got.transpose(2, 1, 0)).reshape(1, S, D)


def _arrays(x, p, positions, norm_g, conv_w_in, conv_dw, conv_dw_b, conv_ln_g, conv_ln_b, conv_w_out, attn_w_in,
            attn_q_norm, attn_k_norm, attn_w_out, ple_w_proj, ple_norm_g, ple_w_gate, ffn1_norm_2, ffn1_w_gate_2,
            ffn1_w_up_2, ffn1_w_down_2, mix_norm_2, w_in_2, q_norm_2, k_norm_2, idx_k_norm_2, conv_w_2, conv_b_2,
            w_mq_2, w_mk_2, b_i_2, b_f_2, m_head_norm_2, w_proj_a_2, w_proj_b_2, w_out_2, ffn2_norm_2,
            ffn2_w_gate_2, ffn2_w_up_2, ffn2_w_down_2):
    f = np.float32
    weights = np.zeros((N_TILES, P, D), f)
    at = [0]

    def put(tiles):
        n, width = len(tiles), tiles.reshape(len(tiles), P, -1).shape[2]
        weights[at[0]:at[0] + n, :, :width] = tiles.reshape(n, P, width)
        at[0] += n

    def paired(a, b):
        return np.stack([_tiles(a), _tiles(b)], axis=1).reshape(-1, P, a.shape[0])

    def wide(w):
        t = _tiles(w)
        per = KC // t.shape[2]
        return t.reshape(-1, per, P, t.shape[2], P).transpose(0, 2, 1, 3, 4)

    def long(w):
        t = _tiles(w)
        full = np.zeros((t.shape[0], P, 3 * KC, P), f)
        full[:, :, :t.shape[2]] = t
        return full.reshape(t.shape[0], P, 3, D).transpose(0, 2, 1, 3).reshape(-1, P, D)

    def ffn(gate, up, down):
        put(paired(gate[0], up[0]))
        put(long(down[0]))

    w = conv_w_in[0]
    put(paired(w[:, 0:D], w[:, D:2 * D]))
    put(_tiles(w[:, 2 * D:3 * D]))
    put(_tiles(conv_w_out[0]))
    put(wide(ple_w_proj[0]))
    put(_tiles(ple_w_gate[0]))
    t = _tiles(attn_w_in[0])
    put(np.stack([t[n] for c in range(4) for n in [s + 4 * g + c for g in range(3) for s in (0, 12, 24)] + [36 + c]]))
    put(wide(attn_w_out[0]))
    put(wide(ple_w_proj[1]))
    put(_tiles(ple_w_gate[1]))
    ffn(ffn1_w_gate_2, ffn1_w_up_2, ffn1_w_down_2)
    w = w_in_2[0]
    q, kk, v, iq, ik, iw, mx, mv, mi, mf, mo, ga, gb = np.split(
        w, np.cumsum([512, 128, 128, 512, 64, 8, 512, 512, 4, 4, 512, D]), axis=1)
    put(_tiles(mx))
    put(_tiles(mv))
    put(_tiles(mo))
    small = np.zeros((D, P), f)
    small[:, 0:8], small[:, 32:36], small[:, 64:68] = iw, mi, mf
    put(_tiles(small))
    heads = [64 * h + d for c in range(4) for h in (c, c + 4) for d in range(64)]
    put(_tiles(q[:, heads]))
    put(_tiles(iq))
    put(_tiles(kk))
    put(_tiles(v))
    put(_tiles(np.concatenate([ik, ik], axis=1)))
    ta, tb, wa, wb = _tiles(ga), _tiles(gb), wide(w_proj_a_2[0][heads]), wide(w_proj_b_2[0])
    for m in range(4):
        for g, pr in ((ta, wa), (tb, wb)):
            put(g[2 * m:2 * m + 2])
            put(pr[m:m + 1])
    put(_tiles(w_out_2[0]))
    ffn(ffn2_w_gate_2, ffn2_w_up_2, ffn2_w_down_2)
    assert at[0] == N_TILES

    params = np.zeros((P, NPARAM), f)

    def param(name, v):
        params[:v.shape[0], PARAMS[name]:PARAMS[name] + v.shape[1]] = v

    param("norm_g0", _cols(norm_g[0]))
    param("norm_g1", _cols(norm_g[1]))
    param("ple_g0", _cols(ple_norm_g[0]))
    param("ple_g1", _cols(ple_norm_g[1]))
    taps = np.concatenate([conv_dw[0], conv_dw_b[0][None]])
    param("taps", taps.reshape(32, KC, P).transpose(2, 1, 0).reshape(P, -1))
    param("ln_g", _cols(conv_ln_g[0]))
    param("ln_b", _cols(conv_ln_b[0]))
    for name, v in (("q_norm", attn_q_norm), ("k_norm", attn_k_norm), ("q_norm2", q_norm_2), ("k_norm2", k_norm_2),
                    ("idx_norm", idx_k_norm_2)):
        param(name, np.concatenate([v[0], v[0]])[:, None])
    param("ffn1", _cols(ffn1_norm_2[0]))
    param("mix", _cols(mix_norm_2[0]))
    param("conv2", conv_w_2[0].reshape(4, 4, P).transpose(2, 1, 0).reshape(P, 16))
    param("conv2_b", _cols(conv_b_2[0]))
    param("m_head", _cols(m_head_norm_2[0]))
    param("ffn2", _cols(ffn2_norm_2[0]))
    param("b_i", b_i_2[0][:, None])
    param("b_f", b_f_2[0][:, None])
    inv = (1.0 / (f(500000.0) ** (np.arange(0, 16, 2, dtype=f) / f(16)))).astype(f)
    freq = np.zeros(HEAD, f)
    freq[0:16] = np.tile(inv, 2)
    param("inv_freq", np.tile(freq, 2)[:, None])
    param("eps", np.full((P, 1), EPS, f))
    param("w_mq", w_mq_2[0].transpose(1, 0, 2).reshape(P, -1))
    param("w_mk", w_mk_2[0].transpose(1, 0, 2).reshape(P, -1))

    r, c = np.arange(P)[:, None], np.arange(P)[None, :]
    rot = np.zeros((P, P), f)
    for h in (0, HEAD):
        for d in range(8):
            rot[h + d + 8, h + d] = -1.0
            rot[h + d, h + d + 8] = 1.0
    pick = np.zeros((P, 4, P), f)
    for h in range(4):
        pick[h, h] = 1.0
    consts = np.concatenate(
        [np.eye(P, dtype=f), np.ones((P, P), f), (r // HEAD == c // HEAD).astype(f), rot,
         np.where((r < 64) & (c >= 64), f(NEG), f(0)), np.where(c < r, f(NEG), f(0)), pick.reshape(P, -1)],
        axis=1).astype(f)

    lq = np.arange(P)[:, None, None]
    res = np.arange(4)[None, :, None]
    key = np.arange(S)[None, None, :]
    dist = 4 * lq + res - key
    near = (dist >= 0) & (dist <= 128)
    lk = np.arange(P)[None, None, :]
    same = np.broadcast_to(lq >= lk, (P, 4, P))
    masks = np.where(np.concatenate([near, same, same & ((lq - lk) % 4 == 0)], axis=2), f(0), f(NEG)).astype(f)
    return {
        "weights": weights,
        "x": np.ascontiguousarray(x[0].reshape(S, KC, P).transpose(2, 1, 0)),
        "ple": np.ascontiguousarray(p[:, 0].reshape(2, S, 2, P).transpose(0, 3, 2, 1)),
        "pos": np.ascontiguousarray(positions),
        "params": params, "consts": consts, "masks": masks,
    }
```

```python
from collections import defaultdict
from contextlib import ExitStack, contextmanager

import numpy as np

import concourse.bass as bass
from concourse import mybir

P = 128
S = 512
D = 1024
KC = D // P
RING = 4
AHEAD = 2
EPS = 1e-6
NEG = -1e30
TAKEN = -3e38
CONV_W = 31
D_FF = 2816
FF = D_FF // P
HEAD = 64
GROUPS = 3
TOPK = 128
POOL_TAP = 22
MH = 4
NQ = S // P

F32 = mybir.dt.float32
F32R = mybir.dt.float32r
I32 = mybir.dt.int32
ALU = mybir.AluOpType
ACT = mybir.ActivationFunctionType
AX = mybir.AxisListType

PARAMS = {}
_at = 0
for _name, _n in (("norm_g0", 8), ("norm_g1", 8), ("ple_g0", 8), ("ple_g1", 8), ("taps", 8 * 32), ("ln_g", 8),
                  ("ln_b", 8), ("q_norm", 1), ("k_norm", 1), ("ffn1", 8), ("mix", 8), ("q_norm2", 1),
                  ("k_norm2", 1), ("idx_norm", 1), ("conv2", 4 * 4), ("conv2_b", 4), ("m_head", 4), ("ffn2", 8),
                  ("b_i", 1), ("b_f", 1), ("inv_freq", 1), ("eps", 1), ("w_mq", 4 * 64), ("w_mk", 4 * 64)):
    PARAMS[_name] = _at
    _at += _n
NPARAM = _at

CONSTS = {"ident": 0, "ones": 128, "head_ones": 256, "rot": 384, "diag_block": 512, "diag_causal": 640,
          "pick": 768}
NCONST = 768 + 4 * P

N_TILES = 24 + 8 + 10 + 40 + 4 + 10 + (2 * FF + 24) + 40 + 8 + 8 + (2 * FF + 24)


READS = (8, 8, 10, 40, 4, 10, FF, 8, 24, 4, 4, 8, FF, 8)
TILES = (24, 8, 10, 40, 4, 10, 2 * FF, 24, 24, 12, 12, 8, 2 * FF, 24)
TILES0 = [0] + [sum(TILES[:n]) for n in range(14)]
READ0 = [0] + [4 + sum(READS[:n]) for n in range(14)]
PI = 3.1415925
ROUND = 1.5 * 2.0 ** 23
TURN = (6.28125, 0.0019350051879882812, 3.019916e-07)


class Counts:

    def __init__(self):
        self.n, self.rate, self.i = defaultdict(int), {}, None

    def at(self, sem, off=0):
        v = self.n.get(sem, 0) + off
        if self.i is not None and self.rate.get(sem, 0):
            if v <= 0 and not isinstance(sem, str):
                raise ValueError(f"a wait in a loop against {v}: {sem.name}")
            return self.i * self.rate[sem] + v
        return v

    def up(self, sem, by=1):
        self.n[sem] = self.n.get(sem, 0) + by
        return self.at(sem)

    @contextmanager
    def repeat(self, eng, times, rates):
        before = dict(self.n)
        self.rate = rates
        with eng.Fori(0, times) as i:
            self.i = i
            yield i
        self.i = None
        made = {s: v - before.get(s, 0) for s, v in self.n.items() if v != before.get(s, 0)}
        if made != {s: r for s, r in rates.items() if r}:
            raise ValueError("rates: " + str({(s if isinstance(s, str) else s.name): r for s, r in made.items()}))
        for s, r in made.items():
            self.n[s] = before.get(s, 0) + r * times


SLOTS = 10
QK_TILES = (0, 1, 3, 4, 6, 7)
SUM_SLOT = {t + 1: n for n, t in enumerate(QK_TILES)}
ROT_SLOT = {t + 2: n for n, t in enumerate(QK_TILES)}
V_SLOT = {3 * g + 3: g for g in range(GROUPS)}
UNITS = 8
KVI_TILES = 3
HEAD_SUMS = {1: ("c", 0), 2: ("c", 1), 3: ("h", 0), 4: ("c", 2), 5: ("c", 3), 6: ("h", 1), 7: ("c", 4),
             8: ("c", 5), 9: ("h", 2), 12: ("h", 3)}
DSA_TILES = 11
TIMES = {"chunk": 4 * len(QK_TILES), "unit": 4 * UNITS}


def build(nc, weights, x_in, ple_in, pos_in, params_in, consts_in, masks_in, out):
    ctx = ExitStack()
    with ctx:
        def sb(name, shape, dt=F32):
            return ctx.enter_context(nc.sbuf_tensor(name, shape, dt))

        def sem(name):
            return ctx.enter_context(nc.semaphore(name))

        X = sb("X", [P, KC, S])
        H_hi = sb("H_hi", [P, KC, S], F32R)
        H_lo = sb("H_lo", [P, KC, S], F32R)
        w_raw = sb("w_raw", [P, RING, D])
        w_hi = sb("w_hi", [P, RING, D], F32R)
        w_lo = sb("w_lo", [P, RING, D], F32R)
        par = sb("par", [P, NPARAM])
        con = sb("con", [P, NCONST])
        sq = sb("sq", [P, 2, S])
        tmp = sb("tmp", [P, 2, S])
        var = sb("var", [P, S])
        r0 = sb("r0", [P, S])
        rs = sb("rs", [P, S])
        ps = ctx.enter_context(nc.psum_tensor("ps", [P, 8, S], F32))

        def const(name, n=P):
            return con[:, CONSTS[name]:CONSTS[name] + n]

        def col(name, j=0, n=1):
            return par[:, PARAMS[name] + j:PARAMS[name] + j + n]

        ident = const("ident")
        ones = const("ones")
        head_ones = const("head_ones")

        def scope(*specs):
            with ExitStack() as s:
                return [s.enter_context(nc.sbuf_tensor(n, sh, dt)) for n, sh, dt in specs]

        pl_raw, pl_hi, pl_lo, pl_P, cv_Y, cv_G, cv_sg, cv_a, cv_acc, cv_pool, cv_w, cv_prod = scope(
            ("pl_raw", [P, 2, S], F32), ("pl_hi", [P, 2, S], F32R), ("pl_lo", [P, 2, S], F32R),
            ("pl_P", [P, KC, S], F32), ("cv_Y", [P, KC, S], F32), ("cv_G", [P, KC, S], F32),
            ("cv_sg", [P, 2, S], F32), ("cv_a", [P, 2, S], F32), ("cv_acc", [P, 2, S], F32),
            ("cv_pool", [P, 2, S], F32), ("cv_w", [P, 4, 32], F32),
            ("cv_prod", [P, 2, S], F32))
        (at_raw, at_ab, at_mask, at_C, at_S, at_G, at_vT, at_SG, at_Sm, at_PT, at_st, at_Yh, at_Yl, at_V) = scope(
            ("at_raw", [P, 12, S], F32), ("at_ab", [P, 2, S], F32), ("at_mask", [P, 4, 768], F32),
            ("at_C", [P, S], F32), ("at_S", [P, S], F32), ("at_G", [P, 4, P], F32), ("at_vT", [P, S], F32),
            ("at_SG", [P, 2, S], F32), ("at_Sm", [P, 768], F32), ("at_PT", [P, 768], F32),
            ("at_st", [P, 4, 4], F32), ("at_Yh", [P, 4, S], F32R), ("at_Yl", [P, 4, S], F32R), ("at_V", [P, 6, S], F32))
        mid_hi, mid_lo = scope(("mid_hi", [P, FF, S], F32R), ("mid_lo", [P, FF, S], F32R))
        m_hi, m_lo = scope(("m_hi", [P, KC, S], F32R), ("m_lo", [P, KC, S], F32R))
        with ExitStack() as s_mix:
            def keep(n, sh, dt):
                return s_mix.enter_context(nc.sbuf_tensor(n, sh, dt))
            yb_hi, yb_lo = keep("yb_hi", [P, 4, S], F32R), keep("yb_lo", [P, 4, S], F32R)
            IW = keep("IW", [P, NQ, 8], F32)
            ds_U = keep("ds_U", [P, 8, S], F32)
            ds_kvi = keep("ds_kvi", [P, 3, S], F32)
            with ExitStack() as s_ml:
                ml_U, ml_k, ml_m, ml_h, ml_EB, ml_cT = [s_ml.enter_context(nc.sbuf_tensor(n, sh, F32)) for n, sh in (
                    ("ml_U", [P, 12, S]), ("ml_k", [HEAD, MH, S]), ("ml_m", [4, 2, S]), ("ml_h", [P, S]),
                    ("ml_EB", [P, S]), ("ml_cT", [P, NQ, 4]))]
                ml_sm, ml_g = scope(("ml_sm", [P, S], F32), ("ml_g", [4, 4, S], F32))
                ml_NM, ml_NMd, ml_E = scope(("ml_NM", [P, S], F32), ("ml_NMd", [P, NQ, P], F32),
                                            ("ml_E", [P, 10 * P], F32))
            ya_hi, ya_lo = keep("ya_hi", [P, 4, S], F32R), keep("ya_lo", [P, 4, S], F32R)
            mb = keep("mb", [P, KC, S], F32)
            (ds_acc, ds_bias, ds_P, ds_PT, ds_st, ds_mx) = scope(
                ("ds_acc", [P, S], F32), ("ds_bias", [P, NQ - 1, S], F32), ("ds_P", [P, 2, S], F32),
                ("ds_PT", [P, 2, S], F32), ("ds_st", [P, 32, 4], F32), ("ds_mx", [P, 8], F32))
            mg_s, mg_t = scope(("mg_s", [P, 2, S], F32), ("mg_t", [P, 2, S], F32))

        landed = [sem(f"landed{i}") for i in range(RING)]
        x_loaded = [sem(f"x_loaded{q}") for q in range(4)]
        par_loaded, con_loaded, ple_loaded, mask_loaded, pos_loaded = (sem(n) for n in (
            "par_loaded", "con_loaded", "ple_loaded", "mask_loaded", "pos_loaded"))
        stored = sem("stored")
        hi_done = sem("hi_done")
        lo_done = sem("lo_done")
        tile_done = sem("tile_done")
        read_out = sem("read_out")
        ended = {e: sem(f"ended_{e}") for e in ("act", "dve", "pe", "pool")}
        act_chain = sem("act_chain")
        dve_chain = sem("dve_chain")
        gated = sem("gated")
        sq_done = sem("sq_done")
        sq_used = sem("sq_used")
        r0_done = sem("r0_done")
        x_squared = sem("x_squared")
        x_summed = sem("x_summed")
        gate_out = sem("gate_out")
        prod_done = sem("prod_done")
        prod_used = sem("prod_used")
        rs_done = sem("rs_done")
        tmp_done = sem("tmp_done")
        split_hi = sem("split_hi")
        split_lo = sem("split_lo")
        act_out = sem("act_out")
        dve_out = sem("dve_out")
        pe_out = sem("pe_out")
        pool_out = sem("pool_out")
        rot_done = sem("rot_done")
        n_done = sem("n_done")
        s_done = sem("s_done")
        m_done = sem("m_done")
        e_done = sem("e_done")
        p_done = sem("p_done")
        t_done = sem("t_done")
        pt_done = sem("pt_done")
        o_done = sem("o_done")
        v_turned = sem("v_turned")
        v_copied = sem("v_copied")
        small_turned = sem("small_turned")
        small_copied = sem("small_copied")
        angles_done = sem("angles_done")
        pool_chain = sem("pool_chain")
        gates_in = sem("gates_in")
        logs_done = sem("logs_done")
        gates_done = sem("gates_done")
        conv_done = sem("conv_done")
        xc_done = sem("xc_done")
        qk_made = sem("qk_made")
        qk_copied = sem("qk_copied")
        max_made = sem("max_made")
        max_copied = sem("max_copied")
        diag_done = sem("diag_done")
        decay_done = sem("decay_done")
        kq_made = sem("kq_made")
        kq_done = sem("kq_done")
        sums_made = sem("sums_made")
        h_done = sem("h_done")

        block = ctx.enter_context(nc.Block())

        STAGES = len(TILES)
        followed = {}

        def begin(k, stage):
            k.n[tile_done], k.n[read_out] = TILES0[stage], READ0[stage]

        def stage_end(eng, own, k, stage=None):
            if stage is not None:
                for s, v in k.n.items():
                    if v and s not in (tile_done, read_out, "prep", "tile") and s not in landed:
                        if followed.setdefault((stage, s), v) != v:
                            raise ValueError(f"stage {stage}, {own}: {s.name} {v}, others {followed[stage, s]}")
            eng.drain().then_inc(ended[own], 1)
            k.up(ended[own])
            for other in ended:
                if other != own:
                    eng.wait_ge(ended[other], k.up(ended[other]))

        def dsa_chunk(m):
            if m < 2:
                return ds_kvi[:, m, :], ("k_norm2", "idx_norm")[m]
            return ds_U[:, m - 2, :], "q_norm2"

        def dsa_out(t):
            return ds_kvi[:, t, :] if t < KVI_TILES else ds_U[:, t - KVI_TILES, :]

        def key_block(b):
            at = (0, 512, 1024, 896)[b]
            return slice(at, at + S - P * b)

        V0 = GROUPS * 4

        def attention_over(k, chunk=(), unit=()):
            for kind, sems in (("chunk", chunk), ("unit", unit)):
                for s in sems:
                    k.n[s] = k.n.get(s, 0) + TIMES[kind]

        def bank_of(tile):
            return tile % 4

        def chunk(t, j):
            return t[:, bass.ds(j, 1), :]

        def flat(ap):
            return ap.rearrange("p a b -> p (a b)")

        @block.sync
        def _(sp):
            for u in range(RING):
                sp.dma_start(w_raw[:, u, :], weights[u]).then_inc(landed[u], 16)
            n_tiles = sum(TILES)
            with sp.Fori(1, n_tiles // RING) as i:
                for u in range(RING):
                    sp.wait_ge(lo_done, RING * i + u - RING + 1)
                    sp.dma_start(w_raw[:, u, :], weights[RING * i + u]).then_inc(landed[u], 16)
            for n in range(n_tiles // RING * RING, n_tiles + AHEAD):
                sp.wait_ge(lo_done, n - RING + 1)
                sp.dma_start(w_raw[:, n % RING, :], weights[n % N_TILES]).then_inc(landed[n % RING], 16)
            sp.wait_ge(ended["dve"], STAGES)
            sp.dma_start(out, X[:, :, :]).then_inc(stored, 16)
            sp.wait_ge(stored, 16)

        @block.gpsimd
        def _(pool):
            k = Counts()

            begin(k, 1)
            for _ in range(2):
                pool.drain().then_inc(prod_used, 1)
            for c in range(KC):
                pool.wait_ge(read_out, k.up(read_out))
                for n in range(CONV_W - POOL_TAP):
                    t = POOL_TAP + n
                    o, a = cv_pool[:, c % 2, t:S], cv_prod[:, (c * (CONV_W - POOL_TAP) + n) % 2, 0:S - t]
                    pool.wait_ge(prod_done, (CONV_W - POOL_TAP) * c + n + 1)
                    if n == 0:
                        instr = pool.tensor_copy(o, a)
                    else:
                        pool.wait_ge(prod_used, (CONV_W - POOL_TAP) * c + n + 2)
                        instr = pool.tensor_tensor(o, o, a, ALU.add)
                    instr.then_inc(prod_used, 1)
            for stage in range(1, STAGES + 1):
                if stage == 3:
                    pool.dma_start(at_SG[:, 0, :].bitcast(I32), pos_in.to_broadcast([P, S])).then_inc(pos_loaded, 16)
                    pool.wait_ge(pos_loaded, 16)

                    def link(instr):
                        instr.then_inc(pool_chain, 1)
                        pool.wait_ge(pool_chain, k.up(pool_chain))

                    ang, n, part = at_V[:, 0, :], at_V[:, 1, :], at_V[:, 2, :]
                    link(pool.tensor_copy(part, at_SG[:, 0, :].bitcast(I32)))
                    link(pool.tensor_scalar(ang, part, col("inv_freq"), None, ALU.mult))
                    for dst, turn, shift in ((at_C[:, :], 0.0, 0.0), (at_SG[:, 1, :], 0.25, float(np.pi / 2))):
                        link(pool.tensor_scalar(n, ang, 1.0 / (2 * np.pi), turn, ALU.mult, ALU.add))
                        link(pool.tensor_scalar(n, n, ROUND, None, ALU.add))
                        link(pool.tensor_scalar(n, n, ROUND, None, ALU.subtract))
                        link(pool.tensor_scalar(part, n, TURN[0], None, ALU.mult))
                        link(pool.tensor_tensor(dst, ang, part, ALU.subtract))
                        link(pool.tensor_scalar(dst, dst, shift, None, ALU.add))
                        for turn_part in TURN[1:]:
                            link(pool.tensor_scalar(part, n, turn_part, None, ALU.mult))
                            link(pool.tensor_tensor(dst, dst, part, ALU.subtract))
                        link(pool.tensor_scalar(dst, dst, PI, -PI, ALU.min, ALU.max))
                    pool.drain().then_inc(angles_done, 1)
                if stage == 4:
                    begin(k, 4)
                    for n in range(TIMES["chunk"]):
                        c, m = divmod(n, len(QK_TILES))
                        pool.wait_ge(read_out, k.at(read_out, 10 * c + QK_TILES[m] + 1))
                        if n:
                            pool.wait_ge(rot_done, n)
                        for which, table in enumerate((at_C, at_S)):
                            instr = pool.tensor_tensor(at_ab[:, which, :], at_raw[:, 6 * (c % 2) + m, :], table[:, :],
                                                       ALU.mult)
                        instr.then_inc(pool_out, 1)
                stage_end(pool, "pool", k, stage)

        @block.scalar
        def _(act):
            k = Counts()
            k.up(x_summed)

            def link(instr):
                instr.then_inc(act_chain, 1)
                act.wait_ge(act_chain, k.up(act_chain))

            def copy(out_ap, in_ap):
                return act.activation(out_ap, in_ap, ACT.Copy)

            def prep():
                n = k.n.get("prep", 0)
                s = n % RING
                act.wait_ge(landed[s], k.up(landed[s], 16))
                if n >= RING:
                    act.wait_ge(tile_done, k.at("prep", 1 - RING))
                copy(w_hi[:, s, :], w_raw[:, s, :]).then_inc(hi_done, 1)
                k.up("prep")

            def prep_rates(tiles, **more):
                return {"prep": tiles, **{landed[s]: 4 * tiles for s in range(RING)}}

            def square(src):
                n = k.n.get(sq_done, 0)
                if n >= 2:
                    act.wait_ge(sq_used, k.at(sq_done, -1))
                act.activation(sq[:, n % 2, :], src, ACT.Square).then_inc(sq_done, 1)
                k.up(sq_done)

            def guess(bank, scale, squares=1):
                act.wait_ge(sq_used, k.up(sq_used, squares))
                if k.n.get(r0_done, 0):
                    act.wait_ge(rs_done, k.at(r0_done))
                link(act.activation(r0[:, :], ps[:, bank, :], ACT.Ln, bias=col("eps"), scale=scale))
                act.activation(r0[:, :], r0[:, :], ACT.Exp, scale=-0.5).then_inc(r0_done, 1)
                k.up(r0_done)

            def square_x(m, n=1):
                act.wait_ge(read_out, k.at(read_out))
                act.wait_ge(x_summed, k.at(x_summed))
                out_t = r0[:, :].rearrange("p (a s) -> p a s", a=1) if n == 1 else sq[:, 0:n, :]
                act.activation(out_t, X[:, bass.ds(m, n), :], ACT.Square).then_inc(x_squared, 1)
                k.up(x_squared)
                k.up(x_summed)

            def split(dst, src_slot=None, src=None):
                act.wait_ge(tmp_done, k.up(tmp_done))
                copy(dst, tmp[:, src_slot, :] if src is None else src).then_inc(split_hi, 1)
                k.up(split_hi)

            def norm(src, fresh=False):
                for c in range(KC if fresh else 0):
                    if c % 2 == 0:
                        act.wait_ge(x_loaded[c // 2], 16)
                    square(src[:, c, :])
                guess(4, 1.0 / D, KC if fresh else 1)
                for c in range(KC):
                    split(H_hi[:, c, :], c % 2)

            def ple():
                act.wait_ge(ple_loaded, k.up(ple_loaded, 16))
                copy(pl_hi[:, :, :], pl_raw[:, :, :]).then_inc(act_out, 1)
                k.up(act_out)
                k.up(dve_out)
                guess(4, 1.0 / D)
                prep()
                for c in range(KC):
                    split(H_hi[:, c, :], c % 2)
                prep()
                for half in range(2):
                    act.wait_ge(tile_done, k.up(tile_done))
                    copy(pl_P[:, 4 * half:4 * half + 4, :], ps[:, 4 * half:4 * half + 4, :]).then_inc(read_out, 1)
                    k.up(read_out)
                with k.repeat(act, 2, {tile_done: 4, gated: 4, read_out: 4, x_squared: 4, x_summed: 4,
                                       **prep_rates(4)}) as i:
                    for u in range(4):
                        prep()
                        act.wait_ge(tile_done, k.up(tile_done))
                        act.wait_ge(read_out, k.at(read_out, -1))
                        k.up(read_out)
                        act.activation(sq[:, u % 2, :], ps[:, bank_of(k.n["prep"] - AHEAD - 1), :], ACT.Sigmoid)\
                            .then_inc(gated, 1)
                        k.up(gated)
                        square_x(4 * i + u)

            def adds_to_x(tiles, body, parts=1, squared=True):
                n = body // parts
                rates = {read_out: n, x_squared: n, x_summed: n} if squared else {}
                with k.repeat(act, tiles // body, {**rates, **prep_rates(body)}) as i:
                    for u in range(n):
                        for _ in range(parts):
                            prep()
                        if squared:
                            k.up(read_out)
                            square_x(n * i + u)

            def ffn_up():
                norm(X)
                with k.repeat(act, FF // 2, {tile_done: 4, read_out: 2, gated: 2, split_hi: 2,
                                                    **prep_rates(4)}) as i:
                    for j in range(2):
                        for u in range(2):
                            prep()
                            act.wait_ge(tile_done, k.up(tile_done))
                            if u == 0:
                                act.wait_ge(read_out, k.at(read_out, -1))
                                k.up(read_out)
                                act.activation(sq[:, j, :], ps[:, bank_of(k.n["prep"] - AHEAD - 1), :], ACT.Silu)\
                                    .then_inc(gated, 1)
                                k.up(gated)
                        act.wait_ge(read_out, k.at(read_out))
                        copy(chunk(mid_hi, 2 * i + j), tmp[:, j:j + 1, :]).then_inc(split_hi, 1)
                        k.up(split_hi)

            for q in range(4):
                act.dma_start(X[:, 2 * q:2 * q + 2, :], x_in[:, 2 * q:2 * q + 2, :]).then_inc(x_loaded[q], 16)
            act.dma_start(par[:, :], params_in).then_inc(par_loaded, 16)
            act.dma_start(con[:, :], consts_in).then_inc(con_loaded, 16)
            act.dma_start(pl_raw[:, :, :], ple_in[0]).then_inc(ple_loaded, 16)
            act.wait_ge(par_loaded, 16)
            for _ in range(AHEAD):
                prep()
            begin(k, 1)
            for _ in range(2):
                act.drain().then_inc(gate_out, 1)
            norm(X, fresh=True)
            k.up(gate_out, 2)
            with k.repeat(act, 2, {tile_done: 12, gated: 4, read_out: 4, gate_out: 4, prod_done: 4 * (CONV_W - POOL_TAP),
                                   **prep_rates(12)}) as i:
                def products(j, taps):
                    for t in taps:
                        act.wait_ge(prod_used, k.at(prod_done, 1))
                        slot = (j * (CONV_W - POOL_TAP) + t - POOL_TAP) % 2
                        act.activation(cv_prod[:, slot, 0:S - t], cv_a[:, j % 2, 0:S - t], ACT.Copy,
                                       scale=cv_w[:, j, CONV_W - 1 - t:CONV_W - t]).then_inc(prod_done, 1)
                        k.up(prod_done)

                third = (CONV_W - POOL_TAP) // 3
                for j in range(4):
                    prep()
                    act.wait_ge(tile_done, k.up(tile_done, 2))
                    act.wait_ge(read_out, k.at(read_out, -1))
                    act.activation(cv_sg[:, j % 2, :], ps[:, 3 * (j % 2) + 1, :], ACT.Sigmoid).then_inc(gated, 1)
                    k.up(gated)
                    act.wait_ge(read_out, k.up(read_out))
                    products(j, range(POOL_TAP, POOL_TAP + third))
                    prep()
                    act.wait_ge(tile_done, k.up(tile_done))
                    b = 3 * (j % 2) + 2
                    act.activation(chunk(cv_G, 4 * i + j), ps[:, b:b + 1, :], ACT.Silu).then_inc(gate_out, 1)
                    k.up(gate_out)
                    products(j, range(POOL_TAP + third, POOL_TAP + 2 * third))
                    prep()
                    products(j, range(POOL_TAP + 2 * third, CONV_W))
            k.n[prod_done] = 0
            stage_end(act, "act", k, 1)
            begin(k, 2)
            k.up(pe_out)
            for c in range(KC):
                act.wait_ge(n_done, k.up(n_done))
                square(cv_Y[:, c, :])
            guess(4, 1.0 / D, KC)
            for c in range(KC + 1):
                if c < KC:
                    act.wait_ge(tmp_done, k.up(tmp_done))
                    act.activation(sq[:, c % 2, :], tmp[:, c % 2, :], ACT.Silu, bias=col("ln_b", c))\
                        .then_inc(act_out, 1)
                    k.up(act_out)
                if c:
                    split(H_hi[:, c - 1, :], src=cv_Y[:, c - 1, :])
            adds_to_x(8, 4)
            stage_end(act, "act", k, 2)
            begin(k, 3)
            ple()
            act.wait_ge(angles_done, 1)
            link(act.activation(at_S[:, :], at_C[:, :], ACT.Sin))
            act.activation(at_C[:, :], at_SG[:, 1, :], ACT.Sin)
            stage_end(act, "act", k, 3)
            begin(k, 4)
            act.dma_start(at_mask[:, :, :], masks_in).then_inc(mask_loaded, 16)
            k.up(dve_out)
            norm(X)
            for c in range(5):
                a = c - 1
                for j in range(SLOTS):
                    if c < 4:
                        prep()
                    if a >= 0 and 0 <= j - 2 < UNITS:
                        act.wait_ge(t_done, UNITS * a + j - 1)
                        copy(at_PT[:, :], flat(ps[:, 4:6, :])[:, 0:768]).then_inc(pt_done, 1)
                    if a >= 0 and 0 <= j - 1 < UNITS:
                        act.wait_ge(m_done, UNITS * a + j)
                        st = at_st[:, (j - 1) % 4, :]
                        act.activation(at_Sm[:, :], at_Sm[:, :], ACT.Exp, bias=st[:, 1:2], accum_out=st[:, 2:3])\
                            .then_inc(e_done, 1)
                    v = V_SLOT.get(j - 1) if c < 4 else None
                    if j == 0 and a >= 0:
                        v = GROUPS - 1
                    if v is not None:
                        pair = c if j else a
                        act.wait_ge(v_turned, GROUPS * pair + v + 1)
                        copy(at_V[:, 3 * (pair % 2) + v, :], ps[:, 1, :]).then_inc(v_copied, 1)
                    if c < 4 and j - 1 in SUM_SLOT:
                        guess(1, 1.0 / HEAD)
                    if j == 0 and a >= 1:
                        split(at_Yh[:, a - 1, :], a % 2)
                    if c < 4:
                        act.wait_ge(tile_done, k.up(tile_done))
                        k.up(read_out)
                        if j == 9:
                            act.activation(at_SG[:, c % 2, :], ps[:, 0, :], ACT.Silu).then_inc(read_out, 1)
                        elif j % 3 == 2:
                            copy(at_vT[:, :], ps[:, 0, :]).then_inc(read_out, 1)
                        else:
                            raw = at_raw[:, 6 * (c % 2) + QK_TILES.index(j), :]
                            copy(raw, ps[:, 0, :]).then_inc(read_out, 1)
                            act.wait_ge(read_out, k.at(read_out))
                            square(raw)
            split(at_Yh[:, 3, :], 0)
            attention_over(k, unit=(m_done, e_done, t_done, pt_done, o_done), chunk=(n_done,))
            stage_end(act, "act", k, 4)
            begin(k, 5)
            act.dma_start(pl_raw[:, :, :], ple_in[1]).then_inc(ple_loaded, 16)
            for m in range(4):
                prep()
                k.up(read_out)
                square_x(2 * m, 2)
            stage_end(act, "act", k, 5)
            begin(k, 6)
            ple()
            stage_end(act, "act", k, 6)
            begin(k, 7)
            ffn_up()
            stage_end(act, "act", k, 7)
            begin(k, 8)
            adds_to_x(24, 12, parts=3)
            stage_end(act, "act", k, 8)
            begin(k, 9)
            norm(X)
            for t in range(13):
                if t == 2:
                    act.wait_ge(small_turned, 1)
                    act.activation(IW[:, :, :], ps[:, 4, :].rearrange("p (b r) -> p b r", r=P)[:, :, 0:8],
                                   ACT.Copy, scale=(HEAD ** -0.5) * (8 ** -0.5)).then_inc(small_copied, 1)
                    act.wait_ge(gates_in, 1)
                    link(act.activation(ml_m[:, 0, :], ml_g[:, 1, :], ACT.Abs))
                    link(act.activation(ml_m[:, 0, :], ml_m[:, 0, :], ACT.Exp, scale=-1.0))
                    act.activation(ml_m[:, 0, :], ml_m[:, 0, :], ACT.Ln, bias=1.0).then_inc(logs_done, 1)
                if 0 <= t - 2 < MH:
                    act.wait_ge(conv_done, t - 1)
                    act.activation(ml_U[:, t - 2, :], ml_h[:, :], ACT.Silu).then_inc(xc_done, 1)
                if 0 <= t - 4 < MH:
                    h = t - 4
                    act.wait_ge(qk_made, h + 1)
                    copy(ml_U[0:HEAD, h, :], ps[0:HEAD, 6, :])
                    copy(ml_k[:, h, :], ps[0:HEAD, 7, :]).then_inc(qk_copied, 1)
                if 0 <= t - 7 < MH:
                    h = t - 7
                    act.wait_ge(v_turned, V0 + h + 1)
                    copy(ml_U[:, 4 + h, :], ps[:, 5, :]).then_inc(v_copied, 1)
                if t == 10:
                    act.wait_ge(small_turned, 2)
                    copy(ml_cT[:, :, :], ps[:, 4, 0:16].rearrange("p (b h) -> p b h", h=4)).then_inc(small_copied, 1)
                prep()
                act.wait_ge(tile_done, k.up(tile_done))
                src = ps[:, bank_of(k.n["prep"] - AHEAD - 1), :]
                out_t = ml_sm[:, :] if t == 0 else ml_U[:, t - 1, :]
                act.activation(out_t, src, ACT.Copy if t < 9 else ACT.Sigmoid).then_inc(read_out, 1)
                k.up(read_out)
            for s_ in range(15):
                h, phase = divmod(s_, 3)
                if phase == 0 and h:
                    act.wait_ge(h_done, h)
                    square(ml_h[:, :])
                if phase == 1 and h < MH:
                    act.wait_ge(max_made, h + 1)
                    copy(ml_NM[:, :], ps[:, 5, :])
                    act.activation(ml_EB[:, :], ps[:, 4, :], ACT.Exp).then_inc(max_copied, 1)
                    act.wait_ge(max_copied, h + 1)
                    act.wait_ge(diag_done, h + 1)
                    for b in range(NQ):
                        at = key_block(b)
                        last = act.activation(ml_E[:, at.start:at.start + P], ml_NMd[:, b, :], ACT.Exp,
                                              bias=ml_cT[:, b, h:h + 1])
                        if b < NQ - 1:
                            last = act.activation(ml_E[:, at.start + P:at.stop], ml_NM[:, P * (b + 1):S], ACT.Exp,
                                                  bias=ml_cT[:, b, h:h + 1])
                        last.then_inc(decay_done, 1)
                if s_ - 1 in HEAD_SUMS:
                    kind, _ = HEAD_SUMS[s_ - 1]
                    guess(7, 1.0 / (P if kind == "h" else HEAD))
                if phase == 2 and h:
                    split(yb_hi[:, h - 1, :], 1)
                if s_ == 11:
                    act.wait_ge(v_turned, V0 + MH + 1)
                    copy(ds_kvi[:, 2, :], ps[:, 7, :]).then_inc(v_copied, 1)
                if s_ < DSA_TILES:
                    prep()
                    act.wait_ge(tile_done, k.up(tile_done))
                    copy(dsa_out(s_), ps[:, (s_ + 1) % 2, :]).then_inc(read_out, 1)
                    k.up(read_out)
                    if s_ + 1 in HEAD_SUMS and HEAD_SUMS[s_ + 1][0] == "c":
                        act.wait_ge(read_out, k.at(read_out))
                        square(dsa_out(s_))
            k.up(n_done, 6)
            stage_end(act, "act", k, 9)
            begin(k, 10)
            def gate():
                act.wait_ge(tile_done, k.up(tile_done, 3))
                act.activation(sq[:, 0:2, :], ps[:, 0:2, :], ACT.Sigmoid).then_inc(gated, 1)
                k.up(gated)

            for b in range(1, NQ):
                for h in range(8):
                    if b == 1 and h in (2, 4, 6):
                        prep()
                    act.wait_ge(pe_out, k.up(pe_out))
                    if h >= 2 or b > 1:
                        act.wait_ge(dve_out, k.up(dve_out))
                    act.activation(ds_P[:, h % 2, 0:P * (b + 1)], ps[:, 4 + h % 2, 0:P * (b + 1)], ACT.Relu)\
                        .then_inc(act_out, 1)
                    k.up(act_out)
                if b == 1:
                    gate()
                for _ in range(3):
                    prep()
                gate()
            k.up(dve_out, 2)
            units = [(c, half, b) for c in range(4) for half in range(2) for b in range(NQ)]

            def exps(u):
                n = P * (units[u][2] + 1)
                act.wait_ge(m_done, k.up(m_done))
                act.activation(ds_P[:, u % 2, 0:n], ds_P[:, u % 2, 0:n], ACT.Exp, bias=ds_st[:, u, 1:2],
                               accum_out=ds_st[:, u, 2:3]).then_inc(e_done, 1)
                k.up(e_done)

            exps(0)
            for u in range(32):
                if u < 31:
                    exps(u + 1)
                n = P * (units[u][2] + 1)
                act.wait_ge(t_done, k.up(t_done))
                if u >= 2:
                    act.wait_ge(o_done, k.up(o_done))
                copy(ds_PT[:, u % 2, 0:n], ps[:, 6 + u % 2, 0:n]).then_inc(pt_done, 1)
                k.up(pt_done)
                if u % 8 == 0 and u:
                    act.wait_ge(o_done, k.at(o_done, 1))
                    copy(ya_hi[:, u // 8 - 1, :], ps[:, (u // 8 - 1) % 2, :]).then_inc(split_hi, 1)
                    k.up(split_hi)
            k.up(o_done, 2)
            act.wait_ge(o_done, k.at(o_done))
            copy(ya_hi[:, 3, :], ps[:, 1, :]).then_inc(split_hi, 1)
            k.up(split_hi)
            stage_end(act, "act", k, 10)
            begin(k, 11)
            for m in range(4):
                for _ in range(3):
                    prep()
                act.wait_ge(tile_done, k.up(tile_done, 3))
                act.activation(mg_s[:, :, :], ps[:, 4 * (m % 2):4 * (m % 2) + 2, :], ACT.Sigmoid).then_inc(gated, 1)
                k.up(gated)
                act.wait_ge(tmp_done, k.up(tmp_done))
                copy(m_hi[:, 2 * m:2 * m + 2, :], mg_t[:, :, :]).then_inc(split_hi, 1)
                k.up(split_hi)
            stage_end(act, "act", k, 11)
            begin(k, 12)
            adds_to_x(8, 4)
            stage_end(act, "act", k, 12)
            begin(k, 13)
            ffn_up()
            stage_end(act, "act", k, 13)
            begin(k, 14)
            adds_to_x(24, 12, parts=3, squared=False)
            stage_end(act, "act", k, 14)

        @block.vector
        def _(dve):
            k = Counts()
            k.up(x_summed)

            def link(instr):
                instr.then_inc(dve_chain, 1)
                dve.wait_ge(dve_chain, k.up(dve_chain))

            def prep():
                n = k.n.get("prep", 0)
                s = n % RING
                dve.wait_ge(hi_done, k.up(hi_done))
                dve.tensor_tensor(w_lo[:, s, :], w_raw[:, s, :], w_hi[:, s, :].bitcast(F32), ALU.subtract)\
                    .then_inc(lo_done, 1)
                k.up("prep")

            def prep_rates(tiles):
                return {"prep": tiles, hi_done: tiles}

            def newton(bank, scale, squares=1):
                k.up(sq_used, squares)
                dve.wait_ge(r0_done, k.up(r0_done))
                link(dve.tensor_scalar(var[:, :], ps[:, bank, :], scale, EPS, ALU.mult, ALU.add))
                link(dve.tensor_tensor(rs[:, :], r0[:, :], r0[:, :], ALU.mult))
                link(dve.scalar_tensor_tensor(rs[:, :], rs[:, :], -0.5, var[:, :], ALU.mult, ALU.mult))
                dve.scalar_tensor_tensor(rs[:, :], rs[:, :], 1.5, r0[:, :], ALU.add, ALU.mult).then_inc(rs_done, 1)
                dve.wait_ge(rs_done, k.up(rs_done))

            def sum_x(n=1):
                dve.wait_ge(x_squared, k.up(x_squared))
                for j in range(n):
                    src = r0[:, :] if n == 1 else sq[:, j, :]
                    instr = dve.tensor_tensor(var[:, :], var[:, :], src, ALU.add)
                    if j < n - 1:
                        link(instr)
                instr.then_inc(x_summed, 1)
                dve.wait_ge(x_summed, k.up(x_summed))

            def split(dst, src, hi):
                dve.wait_ge(split_hi, k.up(split_hi))
                dve.tensor_tensor(dst, src, hi.bitcast(F32), ALU.subtract).then_inc(split_lo, 1)
                k.up(split_lo)

            def norm(src, gain, squares=1):
                newton(4, 1.0 / D, squares)
                for c in range(KC + 1):
                    if c < KC:
                        if c >= 2:
                            dve.wait_ge(split_lo, k.at(split_lo))
                        dve.scalar_tensor_tensor(tmp[:, c % 2, :], src[:, c, :], col(gain, c), rs[:, :], ALU.mult,
                                                 ALU.mult).then_inc(tmp_done, 1)
                        k.up(tmp_done)
                    if c:
                        split(H_lo[:, c - 1, :], tmp[:, (c - 1) % 2, :], H_hi[:, c - 1, :])

            def ple(gain):
                dve.wait_ge(act_out, k.up(act_out))
                dve.tensor_tensor(pl_lo[:, :, :], pl_raw[:, :, :], pl_hi[:, :, :].bitcast(F32), ALU.subtract)\
                    .then_inc(dve_out, 1)
                k.up(dve_out)
                k.up(read_out, 2)
                prep()
                norm(X, gain)
                prep()
                link(dve.memset(var[:, :], 0.0))
                with k.repeat(dve, 2, {gated: 4, read_out: 4, dve_chain: 4, x_squared: 4, x_summed: 4,
                                       **prep_rates(4)}) as i:
                    for u in range(4):
                        prep()
                        dve.wait_ge(gated, k.up(gated))
                        m = 4 * i + u
                        v = slice(u % 2, u % 2 + 1)
                        dve.wait_ge(read_out, k.at(read_out, -1))
                        link(dve.tensor_tensor(tmp[:, v, :], sq[:, v, :], chunk(pl_P, m), ALU.mult))
                        dve.tensor_tensor(chunk(X, m), chunk(X, m), tmp[:, v, :], ALU.add).then_inc(read_out, 1)
                        k.up(read_out)
                        sum_x()

            def adds_to_x(tiles, body, parts, scale, squared=True):
                n = body // parts
                rates = {x_squared: n, x_summed: n} if squared else {}
                if squared:
                    link(dve.memset(var[:, :], 0.0))
                with k.repeat(dve, tiles // body, {tile_done: body, **rates, **prep_rates(body)}) as i:
                    for u in range(n):
                        for _ in range(parts):
                            prep()
                        dve.wait_ge(tile_done, k.up(tile_done, parts))
                        bank = bank_of(k.n["prep"] - AHEAD - 1) if parts == 1 else u
                        x = chunk(X, n * i + u)
                        dve.scalar_tensor_tensor(x, ps[:, bank:bank + 1, :], scale, x, ALU.mult, ALU.add)\
                            .then_inc(read_out, 1)
                        if squared:
                            sum_x()

            def ffn_up(gain):
                norm(X, gain)
                with k.repeat(dve, FF // 2, {gated: 2, split_hi: 2, split_lo: 2, tile_done: 4,
                                             **prep_rates(4)}) as i:
                    for j in range(2):
                        prep()
                        prep()
                        dve.wait_ge(gated, k.up(gated))
                        dve.wait_ge(tile_done, k.up(tile_done, 2))
                        b = bank_of(k.n["prep"] - AHEAD - 1)
                        dve.tensor_tensor(tmp[:, j, :], sq[:, j, :], ps[:, b, :], ALU.mult).then_inc(read_out, 1)
                        split(chunk(mid_lo, 2 * i + j), tmp[:, j:j + 1, :], chunk(mid_hi, 2 * i + j))

            for _ in range(4):
                dve.drain().then_inc(read_out, 1)
            dve.drain().then_inc(x_summed, 1)
            dve.wait_ge(par_loaded, 16)
            for q in range(4):
                dve.wait_ge(x_loaded[q], 16)
            for _ in range(AHEAD):
                prep()
            begin(k, 1)
            norm(X, "norm_g0", squares=KC)
            k.up(prod_used, 2)
            with k.repeat(dve, 2, {gated: 4, read_out: 4, prod_used: 4 * (CONV_W - POOL_TAP), dve_chain: 4 * (POOL_TAP + 2) + 1,
                                   **prep_rates(12)}) as i:
                link(dve.tensor_copy(flat(cv_w[:, :, :]), par[:, bass.ds(128 * i + PARAMS["taps"], 128)]))
                for j in range(4):
                    prep()
                    dve.wait_ge(gated, k.up(gated))
                    a = cv_a[:, j % 2, :]
                    dve.tensor_tensor(a, ps[:, 3 * (j % 2), :], cv_sg[:, j % 2, :], ALU.mult).then_inc(read_out, 1)
                    dve.wait_ge(read_out, k.up(read_out))
                    for t in range(POOL_TAP):
                        w = cv_w[:, j, CONV_W - 1 - t:CONV_W - t]
                        acc = cv_acc[:, t % 2, t:S]
                        if t == 0:
                            instr = dve.tensor_scalar(acc, a, w, cv_w[:, j, CONV_W:CONV_W + 1], ALU.mult, ALU.add)
                        elif t == 1:
                            instr = dve.tensor_scalar(acc, a[:, 0:S - t], w, None, ALU.mult)
                        else:
                            dve.wait_ge(dve_chain, k.at(dve_chain, -1))
                            instr = dve.scalar_tensor_tensor(acc, a[:, 0:S - t], w, acc, ALU.mult, ALU.add)
                        instr.then_inc(dve_chain, 1)
                        k.up(dve_chain)
                        if t in (POOL_TAP // 3, 2 * POOL_TAP // 3):
                            prep()
                    dve.wait_ge(dve_chain, k.at(dve_chain))
                    link(dve.tensor_tensor(cv_acc[:, 0, 1:S], cv_acc[:, 0, 1:S], cv_acc[:, 1, 1:S], ALU.add))
                    at = bass.ds(4 * i + j, 1)
                    dve.tensor_copy(cv_Y[:, at, 0:POOL_TAP], cv_acc[:, 0:1, 0:POOL_TAP])
                    dve.wait_ge(prod_used, k.up(prod_used, CONV_W - POOL_TAP))
                    link(dve.tensor_tensor(cv_Y[:, at, POOL_TAP:S], cv_acc[:, 0:1, POOL_TAP:S],
                                           cv_pool[:, j % 2:j % 2 + 1, POOL_TAP:S], ALU.add))
            stage_end(dve, "dve", k, 1)
            begin(k, 2)
            dve.wait_ge(pe_out, k.up(pe_out))
            for c in range(KC):
                dve.scalar_tensor_tensor(cv_Y[:, c, :], ps[:, 5, :], -1.0 / D, cv_Y[:, c, :], ALU.mult, ALU.add)\
                    .then_inc(n_done, 1)
                k.up(n_done)
            newton(4, 1.0 / D, KC)
            for c in range(KC + 2):
                if c < KC:
                    dve.scalar_tensor_tensor(tmp[:, c % 2, :], cv_Y[:, c, :], col("ln_g", c), rs[:, :], ALU.mult,
                                             ALU.mult).then_inc(tmp_done, 1)
                    k.up(tmp_done)
                if 0 <= c - 1 < KC:
                    dve.wait_ge(act_out, k.up(act_out))
                    dve.tensor_tensor(cv_Y[:, c - 1, :], sq[:, (c - 1) % 2, :], cv_G[:, c - 1, :], ALU.mult)\
                        .then_inc(tmp_done, 1)
                    k.up(tmp_done)
                if c >= 2:
                    split(H_lo[:, c - 2, :], cv_Y[:, c - 2, :], H_hi[:, c - 2, :])
            adds_to_x(8, 4, 1, 1.0)
            stage_end(dve, "dve", k, 2)
            begin(k, 3)
            ple("ple_g0")
            stage_end(dve, "dve", k, 3)
            begin(k, 4)
            for j, gain in enumerate(("q_norm", "k_norm")):
                dve.tensor_scalar(at_G[:, 2 * j, :], ident, col(gain), None, ALU.mult)
                dve.tensor_scalar(at_G[:, 2 * j + 1, :], const("rot"), col(gain), None, ALU.mult)
            dve.drain().then_inc(dve_out, 1)
            k.up(dve_out)
            norm(X, "norm_g1")

            def gate(a):
                dve.wait_ge(o_done, UNITS * (a + 1))
                dve.tensor_tensor(tmp[:, (a + 1) % 2, :].rearrange("p (l r) -> p r l", r=4),
                                  ps[:, 6, :].rearrange("p (r l) -> p r l", r=4),
                                  at_SG[:, a % 2, :].rearrange("p (l r) -> p r l", r=4), ALU.mult)\
                    .then_inc(tmp_done, 1)
                k.up(tmp_done)
                split(at_Yl[:, a, :], tmp[:, (a + 1) % 2, :], at_Yh[:, a, :])

            for c in range(5):
                a = c - 1
                for j in range(SLOTS):
                    if j == 0 and a >= 0 or c < 4 and j - 1 in ROT_SLOT:
                        pair, n = (c, ROT_SLOT[j - 1]) if j else (a, len(QK_TILES) - 1)
                        dve.wait_ge(rot_done, len(QK_TILES) * pair + n + 1)
                        dve.tensor_tensor(at_raw[:, 6 * (pair % 2) + n, :], ps[:, 7, :], rs[:, :], ALU.mult)\
                            .then_inc(n_done, 1)
                        dve.wait_ge(n_done, k.up(n_done))
                    if a >= 0 and 0 <= j - 1 < UNITS:
                        u = j - 1
                        st = at_st[:, u % 4, :]
                        if u == 0 and a == 0:
                            dve.wait_ge(mask_loaded, 16)
                        dve.wait_ge(s_done, UNITS * a + u + 1)
                        link(dve.tensor_tensor_reduce(
                            out=at_Sm[:, :], in0=flat(ps[:, 2:4, :])[:, 0:768], in1=at_mask[:, u % 4, :],
                            scale=HEAD ** -0.5, scalar=TAKEN, op0=ALU.add, op1=ALU.max, accum_out=st[:, 0:1]))
                        dve.tensor_scalar(st[:, 1:2], st[:, 0:1], -1.0, None, ALU.mult).then_inc(m_done, 1)
                    if c < 4:
                        prep()
                    if a >= 0 and 0 <= j - 1 < UNITS:
                        dve.wait_ge(e_done, UNITS * a + u + 1)
                        link(dve.reciprocal(st[:, 3:4], st[:, 2:3]))
                        dve.tensor_scalar(at_Sm[:, :], at_Sm[:, :], st[:, 3:4], None, ALU.mult).then_inc(p_done, 1)
                    if c < 4 and j - 1 in SUM_SLOT:
                        newton(1, 1.0 / HEAD)
                    if j == 0 and a >= 1:
                        gate(a - 1)
            gate(3)
            attention_over(k, unit=(s_done, m_done, e_done, p_done, t_done, o_done))
            stage_end(dve, "dve", k, 4)
            begin(k, 5)
            link(dve.memset(var[:, :], 0.0))
            for m in range(4):
                prep()
                dve.wait_ge(tile_done, k.up(tile_done))
                b = 2 * (m % 2)
                dve.tensor_tensor(X[:, 2 * m:2 * m + 2, :], ps[:, b:b + 2, :], X[:, 2 * m:2 * m + 2, :], ALU.add)\
                    .then_inc(read_out, 1)
                sum_x(2)
            stage_end(dve, "dve", k, 5)
            begin(k, 6)
            ple("ple_g1")
            stage_end(dve, "dve", k, 6)
            begin(k, 7)
            ffn_up("ffn1")
            stage_end(dve, "dve", k, 7)
            begin(k, 8)
            adds_to_x(24, 12, 3, 0.5)
            stage_end(dve, "dve", k, 8)
            begin(k, 9)
            norm(X, "mix")
            for t in range(13):
                prep()
                dve.wait_ge(read_out, k.up(read_out))
                if t == 0:
                    dve.tensor_copy(ml_g[:, 0, :], ml_sm[32:36, :])
                    link(dve.tensor_copy(ml_g[:, 1, :], ml_sm[64:68, :]))
                    link(dve.tensor_scalar(ml_g[:, 0, :], ml_g[:, 0, :], par[0:4, PARAMS["b_i"]:PARAMS["b_i"] + 1],
                                           None, ALU.add))
                    dve.tensor_scalar(ml_g[:, 1, :], ml_g[:, 1, :], par[0:4, PARAMS["b_f"]:PARAMS["b_f"] + 1],
                                      None, ALU.add).then_inc(gates_in, 1)
                if 1 <= t <= MH:
                    h = t - 1
                    if h:
                        dve.wait_ge(xc_done, h)
                    link(dve.tensor_scalar(ml_h[:, :], ml_U[:, h, :], col("conv2", 4 * h + 3), col("conv2_b", h),
                                           ALU.mult, ALU.add))
                    for tap in (1, 2, 3):
                        instr = dve.scalar_tensor_tensor(ml_h[:, tap:S], ml_U[:, h, 0:S - tap],
                                                         col("conv2", 4 * h + 3 - tap), ml_h[:, tap:S],
                                                         ALU.mult, ALU.add)
                        if tap < 3:
                            link(instr)
                    instr.then_inc(conv_done, 1)
                if t == 4:
                    dve.wait_ge(logs_done, 1)
                    g = ml_g
                    link(dve.scalar_tensor_tensor(g[:, 1, :], g[:, 1, :], 0.0, ml_m[:, 0, :], ALU.min, ALU.subtract))
                    link(dve.memset(g[:, 3, :], 1.0))
                    link(dve.tensor_tensor_scan(g[:, 2, :], g[:, 3, :], g[:, 1, :], 0.0, ALU.mult, ALU.add))
                    link(dve.tensor_tensor(g[:, 0, :], g[:, 0, :], g[:, 2, :], ALU.subtract))
                    link(dve.tensor_tensor_scan(g[:, 3, :], g[:, 0, :], g[:, 0, :], 0.0, ALU.max, ALU.max))
                    link(dve.tensor_scalar(ml_m[:, 0, :], g[:, 3, :], -1.0, None, ALU.mult))
                    dve.tensor_tensor(ml_m[:, 1, :], ml_m[:, 0, :], g[:, 2, :], ALU.subtract).then_inc(gates_done, 1)
            for s_ in range(15):
                h, phase = divmod(s_, 3)
                if phase == 0 and h:
                    dve.wait_ge(sums_made, h)
                    link(dve.tensor_scalar(tmp[:, 0, :], ps[:, 3, :], -1.0, None, ALU.mult))
                    link(dve.tensor_tensor(tmp[:, 0, :], ps[:, 3, :], tmp[:, 0, :], ALU.max))
                    link(dve.tensor_tensor(tmp[:, 0, :], tmp[:, 0, :], ml_EB[:, :], ALU.max))
                    link(dve.reciprocal(tmp[:, 0, :], tmp[:, 0, :]))
                    dve.tensor_tensor(ml_h[:, :], ps[:, 2, :], tmp[:, 0, :], ALU.mult).then_inc(h_done, 1)
                    dve.wait_ge(h_done, h)
                if phase == 1 and h < MH:
                    dve.wait_ge(max_copied, h + 1)
                    for b in range(NQ):
                        instr = dve.tensor_tensor(ml_NMd[:, b, :], ml_NM[:, b * P:(b + 1) * P],
                                                  const("diag_causal"), ALU.add)
                    instr.then_inc(diag_done, 1)
                if phase == 2 and h < MH:
                    dve.wait_ge(kq_made, h + 1)
                    for b in range(NQ):
                        dve.wait_ge(decay_done, NQ * h + b + 1)
                        at = key_block(b)
                        dve.scalar_tensor_tensor(ml_E[:, at], flat(ps[:, 4:7, :])[:, at], HEAD ** -0.5, ml_E[:, at],
                                                 ALU.mult, ALU.mult).then_inc(kq_done, 1)
                if s_ < DSA_TILES:
                    prep()
                    k.up(read_out)
                if s_ - 1 in HEAD_SUMS:
                    kind, m = HEAD_SUMS[s_ - 1]
                    newton(7, 1.0 / (P if kind == "h" else HEAD))
                    if kind == "c":
                        src, gain = dsa_chunk(m)
                        dve.scalar_tensor_tensor(src, src, col(gain), rs[:, :], ALU.mult, ALU.mult)\
                            .then_inc(n_done, 1)
                        dve.wait_ge(n_done, k.up(n_done))
                    else:
                        link(dve.scalar_tensor_tensor(tmp[:, 0, :], ml_h[:, :], col("m_head", m), rs[:, :],
                                                      ALU.mult, ALU.mult))
                        dve.tensor_tensor(tmp[:, 1, :], tmp[:, 0, :], ml_U[:, 8 + m, :], ALU.mult)\
                            .then_inc(tmp_done, 1)
                        dve.wait_ge(tmp_done, k.up(tmp_done))
                if phase == 2 and h:
                    split(yb_lo[:, h - 1, :], tmp[:, 1, :], yb_hi[:, h - 1, :])
            stage_end(dve, "dve", k, 9)
            begin(k, 10)
            def gate(m):
                dve.wait_ge(gated, k.up(gated))
                dve.tensor_tensor(mb[:, 2 * m:2 * m + 2, :], sq[:, 0:2, :], ps[:, 2:4, :], ALU.mult)\
                    .then_inc(read_out, 1)

            for b in range(1, NQ):
                n = P * (b + 1)
                acc = ds_acc[:, 0:n]
                for h in range(8):
                    if b == 1 and h in (2, 4, 6):
                        prep()
                    dve.wait_ge(act_out, k.up(act_out))
                    if h == 0:
                        instr = dve.tensor_scalar(acc, ds_P[:, 0, 0:n], IW[:, b, 0:1], None, ALU.mult)
                    else:
                        instr = dve.scalar_tensor_tensor(acc, ds_P[:, h % 2, 0:n], IW[:, b, h:h + 1], acc,
                                                         ALU.mult, ALU.add)
                    instr.then_inc(dve_out, 1)
                    dve.wait_ge(dve_out, k.up(dve_out))
                link(dve.tensor_tensor(ds_acc[:, b * P:n], ds_acc[:, b * P:n], const("diag_block"), ALU.add))
                for turn in range(TOPK // 8):
                    if b == 1 and turn == 1:
                        gate(0)
                    if turn in (2, 5, 8):
                        prep()
                    link(dve.max(ds_mx[:, :], acc))
                    link(dve.match_replace(acc, ds_mx[:, :], acc, TAKEN))
                link(dve.tensor_scalar(acc, acc, TAKEN, -NEG, ALU.is_equal, ALU.mult))
                link(dve.tensor_scalar(ds_bias[:, b - 1, 0:n], acc, NEG, None, ALU.add))
                gate(b)
            k.up(pe_out, 24)
            units = [(c, half, b) for c in range(4) for half in range(2) for b in range(NQ)]

            def masked(u):
                b = units[u][2]
                n = P * (b + 1)
                if u >= 2:
                    dve.wait_ge(t_done, k.up(t_done))
                dve.wait_ge(s_done, k.up(s_done))
                bias = const("diag_block") if b == 0 else ds_bias[:, b - 1, 0:n]
                link(dve.tensor_tensor_reduce(out=ds_P[:, u % 2, 0:n], in0=ps[:, 4 + u % 2, 0:n], in1=bias,
                                              scale=HEAD ** -0.5, scalar=TAKEN, op0=ALU.add, op1=ALU.max,
                                              accum_out=ds_st[:, u, 0:1]))
                dve.tensor_scalar(ds_st[:, u, 1:2], ds_st[:, u, 0:1], -1.0, None, ALU.mult).then_inc(m_done, 1)
                k.up(m_done)

            def out_lo(c):
                dve.wait_ge(split_hi, k.up(split_hi))
                dve.tensor_tensor(ya_lo[:, c, :], ps[:, c % 2, :], ya_hi[:, c, :].bitcast(F32), ALU.subtract)\
                    .then_inc(split_lo, 1)
                k.up(split_lo)

            masked(0)
            for u in range(32):
                if u < 31:
                    masked(u + 1)
                n = P * (units[u][2] + 1)
                dve.wait_ge(e_done, k.up(e_done))
                link(dve.reciprocal(ds_st[:, u, 3:4], ds_st[:, u, 2:3]))
                dve.tensor_scalar(ds_P[:, u % 2, 0:n], ds_P[:, u % 2, 0:n], ds_st[:, u, 3:4], None, ALU.mult)\
                    .then_inc(p_done, 1)
                k.up(p_done)
                if u % 8 == 0 and u:
                    out_lo(u // 8 - 1)
            out_lo(3)
            k.up(t_done, 2)
            k.up(o_done, 32)
            stage_end(dve, "dve", k, 10)
            begin(k, 11)
            for m in range(4):
                for _ in range(3):
                    prep()
                dve.wait_ge(gated, k.up(gated))
                dve.tensor_tensor(mg_t[:, :, :], mg_s[:, :, :], ps[:, 4 * (m % 2) + 2:4 * (m % 2) + 4, :], ALU.mult)\
                    .then_inc(read_out, 1)
                dve.wait_ge(read_out, k.up(read_out))
                dve.tensor_tensor(mg_t[:, :, :], mg_t[:, :, :], mb[:, 2 * m:2 * m + 2, :], ALU.add)\
                    .then_inc(tmp_done, 1)
                dve.wait_ge(tmp_done, k.up(tmp_done))
                split(m_lo[:, 2 * m:2 * m + 2, :], mg_t[:, :, :], m_hi[:, 2 * m:2 * m + 2, :])
                dve.wait_ge(split_lo, k.at(split_lo))
            stage_end(dve, "dve", k, 11)
            begin(k, 12)
            adds_to_x(8, 4, 1, 1.0)
            stage_end(dve, "dve", k, 12)
            begin(k, 13)
            ffn_up("ffn2")
            stage_end(dve, "dve", k, 13)
            begin(k, 14)
            adds_to_x(24, 12, 3, 0.5, squared=False)
            stage_end(dve, "dve", k, 14)

        @block.tensor
        def _(pe):
            k = Counts()
            k.up(x_summed)

            def tile(groups, arriving=None):
                s = k.n.get("tile", 0) % RING
                k.up("tile")
                pe.wait_ge(lo_done, k.up(lo_done))
                for bank, first, last, blocks in groups:
                    for n, (b, x_hi, x_lo) in enumerate(blocks):
                        if arriving is not None:
                            pe.wait_ge(split_lo, arriving - KC + 1 + n)
                        wh = w_hi[:, s, b * P:(b + 1) * P]
                        wl = w_lo[:, s, b * P:(b + 1) * P]
                        for q, (w, x) in enumerate(((wh, x_hi), (wh, x_lo), (wl, x_hi))):
                            mm = pe.matmul(ps[:, bank, :], w, x, start=first and n == 0 and q == 0,
                                           stop=last and n == len(blocks) - 1 and q == 2)
                mm.then_inc(tile_done, 1)

            def blocks(hi, lo, n=KC, at=0, first=0):
                return [(first + b, hi[:, at + b, :], lo[:, at + b, :]) for b in range(n)]

            def single(hi, lo, arriving=None):
                pe.wait_ge(read_out, k.at(read_out, -3))
                tile([(bank_of(k.n["tile"]), True, True, blocks(hi, lo))], arriving)
                k.up(read_out)

            def pair(hi, lo, arriving=None):
                pe.wait_ge(read_out, k.at(read_out, -1))
                for n in range(2):
                    tile([(bank_of(k.n["tile"]), True, True, blocks(hi, lo))], None if n else arriving)
                k.up(read_out)

            def sum_squares(c, n, bank=4, lhsT=None):
                pe.wait_ge(sq_done, k.up(sq_done))
                pe.matmul(ps[:, bank, :], ones if lhsT is None else lhsT, sq[:, (k.n[sq_done] - 1) % 2, :],
                          start=c == 0, stop=c == n - 1).then_inc(sq_used, 1)
                k.up(sq_used)

            def norm(fresh=False):
                if fresh:
                    for c in range(KC):
                        sum_squares(c, KC)
                else:
                    pe.wait_ge(x_summed, k.at(x_summed))
                    pe.matmul(ps[:, 4, :], ones, var[:, :], start=True, stop=True).then_inc(sq_used, 1)
                    k.up(sq_used)
                k.up(r0_done)
                k.up(rs_done)
                k.up(split_lo, KC)

            def ple():
                k.up(act_out)
                norm()
                pe.wait_ge(dve_out, k.up(dve_out))
                for half in range(2):
                    if half:
                        pe.wait_ge(rs_done, k.at(rs_done))
                    tile([(4 * half + m, True, True, blocks(pl_hi, pl_lo, n=2, first=2 * m)) for m in range(4)])
                    k.up(read_out)
                pe.wait_ge(read_out, k.at(read_out, -1))
                with k.repeat(pe, 2, {"tile": 4, lo_done: 4, read_out: 4}):
                    for u in range(4):
                        single(H_hi, H_lo, None if u else k.n[split_lo])
                k.up(x_squared, KC)
                k.up(x_summed, KC)

            def down():
                with k.repeat(pe, 2, {"tile": 12, lo_done: 12, read_out: 4}):
                    for m in range(4):
                        pe.wait_ge(read_out, k.at(read_out, -3))
                        for part in range(3):
                            n = min(KC, FF - KC * part)
                            tile([(m, part == 0, part == 2, blocks(mid_hi, mid_lo, n=n, at=KC * part))])
                        k.up(read_out)

            def up():
                norm()
                with k.repeat(pe, FF // 2, {"tile": 4, lo_done: 4, read_out: 2}):
                    for u in range(2):
                        pair(H_hi, H_lo, None if u else k.n[split_lo])
                k.up(split_lo, FF)

            begin(k, 1)
            pe.wait_ge(con_loaded, 16)
            norm(fresh=True)
            k.up(gate_out, 2)
            with k.repeat(pe, 2, {"tile": 12, lo_done: 12, read_out: 4, gate_out: 4}):
                for j in range(4):
                    pe.wait_ge(read_out, k.at(read_out, -1))
                    pe.wait_ge(gate_out, k.at(gate_out, -1))
                    for n in range(3):
                        tile([(3 * (j % 2) + n, True, True, blocks(H_hi, H_lo))],
                             None if j or n else k.n[split_lo])
                    k.up(read_out)
                    k.up(gate_out)
            stage_end(pe, "pe", k, 1)
            begin(k, 2)
            for c in range(KC):
                mm = pe.matmul(ps[:, 5, :], ones, cv_Y[:, c, :], start=c == 0, stop=c == KC - 1)
            mm.then_inc(pe_out, 1)
            k.up(pe_out)
            k.up(n_done, KC)
            norm(fresh=True)
            k.up(act_out, KC)
            with k.repeat(pe, 2, {"tile": 4, lo_done: 4, read_out: 4}):
                for u in range(4):
                    single(H_hi, H_lo, None if u else k.n[split_lo])
            k.up(x_squared, KC)
            k.up(x_summed, KC)
            stage_end(pe, "pe", k, 2)
            begin(k, 3)
            ple()
            stage_end(pe, "pe", k, 3)
            begin(k, 4)
            norm()
            pe.wait_ge(dve_out, k.up(dve_out))
            normed, sums, gated_out = k.n[n_done], k.n[rs_done], k.n[split_lo]
            for c in range(5):
                a = c - 1
                for j in range(SLOTS):
                    if c < 4:
                        pe.wait_ge(read_out, k.at(read_out))
                        tile([(0, True, True, blocks(H_hi, H_lo))], k.n[split_lo] if c == 0 and j == 0 else None)
                        k.up(read_out)
                    if c < 4 and j in ROT_SLOT:
                        n = len(QK_TILES) * c + ROT_SLOT[j]
                        pe.wait_ge(pool_out, n + 1)
                        if n:
                            pe.wait_ge(n_done, normed + n)
                        for which in range(2):
                            mm = pe.matmul(ps[:, 7, :], at_G[:, 2 * (n % 2) + which, :], at_ab[:, which, :],
                                           start=which == 0, stop=which == 1)
                        mm.then_inc(rot_done, 1)
                    if a >= 0 and 0 <= j - 2 < UNITS:
                        u = j - 2
                        rows, r = slice(HEAD * (u // 4), HEAD * (u // 4) + HEAD), u % 4
                        if u == 0:
                            pe.wait_ge(v_copied, GROUPS * (a + 1))
                            if a:
                                pe.wait_ge(split_lo, gated_out + a)
                        pe.wait_ge(pt_done, UNITS * a + u + 1)
                        for b in range(6):
                            g, v = (0, b) if b < 4 else (b - 3, r)
                            mm = pe.matmul(ps[rows, 6, r * P:(r + 1) * P],
                                           at_V[:, 3 * (a % 2) + g, v * P + rows.start:v * P + rows.stop],
                                           at_PT[:, b * P:(b + 1) * P], start=b == 0, stop=b == 5)
                        mm.then_inc(o_done, 1)
                    if a >= 0 and 0 <= j - 1 < UNITS:
                        pe.wait_ge(p_done, UNITS * a + j)
                        for b in range(6):
                            mm = pe.transpose(ps[:, 4 + b // 4, (b % 4) * P:(b % 4 + 1) * P],
                                              at_Sm[:, b * P:(b + 1) * P], ident)
                        mm.then_inc(t_done, 1)
                    if a >= 0 and j < UNITS:
                        rows, r = slice(HEAD * (j // 4), HEAD * (j // 4) + HEAD), j % 4
                        if j == 0:
                            pe.wait_ge(n_done, normed + len(QK_TILES) * (a + 1))
                        elif UNITS * a + j:
                            pe.wait_ge(m_done, UNITS * a + j)
                        q = 6 * (a % 2)
                        pe.matmul(ps[:, 2, :], at_raw[rows, q, r:S:4], at_raw[rows, q + 1, :], start=True, stop=True)
                        for g in (1, 2):
                            mm = pe.matmul(ps[:, 3, (g - 1) * P:g * P], at_raw[rows, q + 2 * g, r:S:4],
                                           at_raw[rows, q + 2 * g + 1, r:S:4], start=True, stop=True)
                        mm.then_inc(s_done, 1)
                    if c < 4 and j in V_SLOT:
                        g = V_SLOT[j]
                        pe.wait_ge(rs_done, sums + len(QK_TILES) * c + 2 * g + 2)
                        for b in range(NQ):
                            v = at_vT[:, b * P:(b + 1) * P] if g == 0 else at_vT[:, b:S:4]
                            mm = pe.transpose(ps[:, 1, b * P:(b + 1) * P], v, ident)
                        mm.then_inc(v_turned, 1)
                    if c < 4 and j in SUM_SLOT:
                        n = len(QK_TILES) * c + SUM_SLOT[j]
                        pe.wait_ge(rs_done, sums + n)
                        if n > 1:
                            pe.wait_ge(v_copied, n // 2)
                        sum_squares(0, 1, 1, head_ones)
            attention_over(k, unit=(s_done, m_done, p_done, t_done, pt_done, o_done), chunk=(r0_done, rs_done, n_done))
            k.up(split_lo, 4)
            stage_end(pe, "pe", k, 4)
            begin(k, 5)
            for m in range(4):
                pe.wait_ge(read_out, k.at(read_out, -1))
                tile([(2 * (m % 2) + n, True, True, blocks(at_Yh, at_Yl, n=4, first=4 * n)) for n in range(2)])
                k.up(read_out)
            k.up(x_squared, 4)
            k.up(x_summed, 4)
            stage_end(pe, "pe", k, 5)
            begin(k, 6)
            ple()
            stage_end(pe, "pe", k, 6)
            begin(k, 7)
            up()
            stage_end(pe, "pe", k, 7)
            begin(k, 8)
            down()
            k.up(x_squared, KC)
            k.up(x_summed, KC)
            stage_end(pe, "pe", k, 8)
            begin(k, 9)
            norm()
            for t in range(13):
                single(H_hi, H_lo, None if t else k.n[split_lo])
                if t == 1:
                    pe.wait_ge(read_out, k.at(read_out, -1))
                    for b in range(NQ):
                        mm = pe.transpose(ps[:, 4, b * P:(b + 1) * P], ml_sm[:, b * P:(b + 1) * P], ident)
                    mm.then_inc(small_turned, 1)
                if 0 <= t - 3 < MH:
                    h = t - 3
                    pe.wait_ge(xc_done, h + 1)
                    if h:
                        pe.wait_ge(qk_copied, h)
                    pe.matmul(ps[0:HEAD, 6, :], col("w_mq", HEAD * h, HEAD), ml_U[:, h, :], start=True, stop=True)
                    pe.matmul(ps[0:HEAD, 7, :], col("w_mk", HEAD * h, HEAD), ml_U[:, h, :], start=True, stop=True)\
                        .then_inc(qk_made, 1)
                if 0 <= t - 6 < MH:
                    h = t - 6
                    pe.wait_ge(read_out, k.at(read_out, -1))
                    if h:
                        pe.wait_ge(v_copied, V0 + h)
                    for b in range(NQ):
                        mm = pe.transpose(ps[:, 5, b * P:(b + 1) * P], ml_U[:, 4 + h, b * P:(b + 1) * P], ident)
                    mm.then_inc(v_turned, 1)
                if t == 9:
                    pe.wait_ge(small_copied, 1)
                    pe.wait_ge(gates_done, 1)
                    for b in range(NQ):
                        mm = pe.transpose(ps[:, 4, 4 * b:4 * b + 4], ml_g[:, 0, b * P:(b + 1) * P], ident[0:4, 0:4])
                    mm.then_inc(small_turned, 1)
            for s_ in range(15):
                h, phase = divmod(s_, 3)
                if s_ < DSA_TILES:
                    pe.wait_ge(read_out, k.at(read_out, -1))
                    tile([((s_ + 1) % 2, True, True, blocks(H_hi, H_lo))])
                    k.up(read_out)
                if phase == 0 and h < MH:
                    if h == 0:
                        pe.wait_ge(small_copied, 2)
                        pe.wait_ge(v_copied, V0 + MH)
                    else:
                        pe.wait_ge(kq_done, NQ * h)
                    for n in range(2):
                        mm = pe.matmul(ps[:, 5 - n, :],
                                       con[0:4, CONSTS["pick"] + P * h:CONSTS["pick"] + P * (h + 1)],
                                       ml_m[:, n, :], start=True, stop=True)
                    mm.then_inc(max_made, 1)
                if phase == 1 and h < MH:
                    pe.wait_ge(max_copied, h + 1)
                    pe.wait_ge(qk_copied, MH)
                    for b in range(NQ):
                        mm = pe.matmul(flat(ps[:, 4:7, :])[:, key_block(b)], ml_k[:, h, b * P:(b + 1) * P],
                                       ml_U[0:HEAD, h, b * P:S], start=True, stop=True)
                    mm.then_inc(kq_made, 1)
                if phase == 2 and h < MH:
                    if h:
                        pe.wait_ge(h_done, h)
                    for b in range(NQ):
                        pe.wait_ge(kq_done, NQ * h + b + 1)
                        for bank, w in ((2, ml_U[:, 4 + h, b * P:(b + 1) * P]), (3, ones)):
                            mm = pe.matmul(ps[:, bank, P * b:S], w, ml_E[:, key_block(b)], start=b == 0,
                                           stop=b == NQ - 1, skip_group_check=True)
                    mm.then_inc(sums_made, 1)
                if s_ == 10:
                    pe.wait_ge(rs_done, k.at(rs_done))
                    for b in range(NQ):
                        mm = pe.transpose(ps[:, 7, b * P:(b + 1) * P], ds_kvi[:, 2, b * P:(b + 1) * P], ident)
                    mm.then_inc(v_turned, 1)
                if s_ in HEAD_SUMS:
                    pe.wait_ge(rs_done, k.at(rs_done))
                    if s_ == 12:
                        pe.wait_ge(v_copied, V0 + MH + 1)
                    sum_squares(0, 1, 7, None if HEAD_SUMS[s_][0] == "h" else head_ones)
                    k.up(rs_done)
                    k.up(r0_done)
            k.up(split_lo, MH)
            k.up(n_done, 6)
            stage_end(pe, "pe", k, 9)
            begin(k, 10)
            def branch(n):
                if n == 0:
                    pe.wait_ge(read_out, k.at(read_out))
                if n < 2:
                    tile([(n, True, True, blocks(H_hi, H_lo))])
                else:
                    tile([(2 + m, True, True, blocks(yb_hi, yb_lo, n=4, first=4 * m)) for m in range(2)])
                    k.up(read_out)

            for b in range(1, NQ):
                for h in range(8):
                    if b == 1 and h in (2, 4, 6):
                        branch(h // 2 - 1)
                    if h >= 2 or b > 1:
                        pe.wait_ge(act_out, k.up(act_out))
                    rows = slice(HEAD * (h % 2), HEAD * (h % 2) + HEAD)
                    pe.matmul(ps[:, 4 + h % 2, 0:P * (b + 1)], ds_U[rows, 4 + h // 2, b * P:(b + 1) * P],
                              ds_kvi[rows, 1, 0:P * (b + 1)], start=True, stop=True).then_inc(pe_out, 1)
                    k.up(pe_out)
                for n in range(3):
                    branch(n)
            pe.wait_ge(read_out, k.at(read_out))
            pe.wait_ge(act_out, k.up(act_out, 2))
            k.up(dve_out, 24)
            units = [(c, half, b) for c in range(4) for half in range(2) for b in range(NQ)]

            def scores(u):
                c, half, b = units[u]
                rows = slice(HEAD * half, HEAD * half + HEAD)
                if u >= 2:
                    pe.wait_ge(m_done, k.up(m_done))
                pe.matmul(ps[:, 4 + u % 2, 0:P * (b + 1)], ds_U[rows, c, b * P:(b + 1) * P],
                          ds_kvi[rows, 0, 0:P * (b + 1)], start=True, stop=True).then_inc(s_done, 1)
                k.up(s_done)

            scores(0)
            scores(1)
            for u in range(33):
                if u < 32:
                    b = units[u][2]
                    pe.wait_ge(p_done, k.up(p_done))
                    for kb in range(b + 1):
                        mm = pe.transpose(ps[:, 6 + u % 2, kb * P:(kb + 1) * P],
                                          ds_P[:, u % 2, kb * P:(kb + 1) * P], ident)
                    mm.then_inc(t_done, 1)
                    k.up(t_done)
                if u < 30:
                    scores(u + 2)
                if u:
                    c, half, b = units[u - 1]
                    rows = slice(HEAD * half, HEAD * half + HEAD)
                    pe.wait_ge(pt_done, k.up(pt_done))
                    if u % 8 == 1 and c >= 2:
                        pe.wait_ge(split_lo, k.at(split_lo, c - 1))
                    for kb in range(b + 1):
                        mm = pe.matmul(ps[rows, c % 2, b * P:(b + 1) * P],
                                       ds_kvi[:, 2, kb * P + rows.start:kb * P + rows.stop],
                                       ds_PT[:, (u - 1) % 2, kb * P:(kb + 1) * P], start=kb == 0, stop=kb == b)
                    mm.then_inc(o_done, 1)
                    k.up(o_done)
            k.up(m_done, 2)
            k.up(split_lo, 4)
            stage_end(pe, "pe", k, 10)
            begin(k, 11)
            for m in range(4):
                pe.wait_ge(read_out, k.at(read_out, -1))
                for n in range(2):
                    tile([(4 * (m % 2) + n, True, True, blocks(H_hi, H_lo))])
                tile([(4 * (m % 2) + 2 + n, True, True, blocks(ya_hi, ya_lo, n=4, first=4 * n)) for n in range(2)])
                k.up(read_out)
            k.up(split_lo, 4)
            stage_end(pe, "pe", k, 11)
            begin(k, 12)
            with k.repeat(pe, 2, {"tile": 4, lo_done: 4, read_out: 4}):
                for _ in range(4):
                    single(m_hi, m_lo)
            k.up(x_squared, KC)
            k.up(x_summed, KC)
            stage_end(pe, "pe", k, 12)
            begin(k, 13)
            up()
            stage_end(pe, "pe", k, 13)
            begin(k, 14)
            down()
            stage_end(pe, "pe", k, 14)


def _tiles(w):
    k, m = w.shape
    return w.reshape(k // P, P, m // P, P).transpose(2, 1, 0, 3)


def _cols(v):
    return np.asarray(v).reshape(-1, P).T


def kernel(x, p, positions, norm_g, conv_w_in, conv_dw, conv_dw_b, conv_ln_g, conv_ln_b, conv_w_out, attn_w_in,
           attn_q_norm, attn_k_norm, attn_w_out, ple_w_proj, ple_norm_g, ple_w_gate, ffn1_norm_2, ffn1_w_gate_2,
           ffn1_w_up_2, ffn1_w_down_2, mix_norm_2, w_in_2, q_norm_2, k_norm_2, idx_k_norm_2, conv_w_2, conv_b_2,
           w_mq_2, w_mk_2, b_i_2, b_f_2, m_head_norm_2, w_proj_a_2, w_proj_b_2, w_out_2, ffn2_norm_2,
           ffn2_w_gate_2, ffn2_w_up_2, ffn2_w_down_2):
    from concourse import bacc
    from concourse.bass_utils import run_bass_kernel_spmd

    arrays = _arrays(x, p, positions, norm_g, conv_w_in, conv_dw, conv_dw_b, conv_ln_g, conv_ln_b, conv_w_out,
                     attn_w_in, attn_q_norm, attn_k_norm, attn_w_out, ple_w_proj, ple_norm_g, ple_w_gate,
                     ffn1_norm_2, ffn1_w_gate_2, ffn1_w_up_2, ffn1_w_down_2, mix_norm_2, w_in_2, q_norm_2,
                     k_norm_2, idx_k_norm_2, conv_w_2, conv_b_2, w_mq_2, w_mk_2, b_i_2, b_f_2, m_head_norm_2,
                     w_proj_a_2, w_proj_b_2, w_out_2, ffn2_norm_2, ffn2_w_gate_2, ffn2_w_up_2, ffn2_w_down_2)
    nc = bacc.Bacc("TRN2", target_bir_lowering=False, num_devices=1)
    args = [nc.dram_tensor(n, a.shape, mybir.dt.from_np(a.dtype), kind="ExternalInput").ap()
            for n, a in arrays.items()]
    out = nc.dram_tensor("out", (P, KC, S), F32, kind="ExternalOutput").ap()
    build(nc, *args, out)
    got = run_bass_kernel_spmd(nc, [arrays], core_ids=[0]).results[0]["out"]
    return np.ascontiguousarray(got.transpose(2, 1, 0)).reshape(1, S, D)


def _arrays(x, p, positions, norm_g, conv_w_in, conv_dw, conv_dw_b, conv_ln_g, conv_ln_b, conv_w_out, attn_w_in,
            attn_q_norm, attn_k_norm, attn_w_out, ple_w_proj, ple_norm_g, ple_w_gate, ffn1_norm_2, ffn1_w_gate_2,
            ffn1_w_up_2, ffn1_w_down_2, mix_norm_2, w_in_2, q_norm_2, k_norm_2, idx_k_norm_2, conv_w_2, conv_b_2,
            w_mq_2, w_mk_2, b_i_2, b_f_2, m_head_norm_2, w_proj_a_2, w_proj_b_2, w_out_2, ffn2_norm_2,
            ffn2_w_gate_2, ffn2_w_up_2, ffn2_w_down_2):
    f = np.float32
    weights = np.zeros((N_TILES, P, D), f)
    at = [0]

    def put(tiles):
        n, width = len(tiles), tiles.reshape(len(tiles), P, -1).shape[2]
        weights[at[0]:at[0] + n, :, :width] = tiles.reshape(n, P, width)
        at[0] += n

    def paired(a, b):
        return np.stack([_tiles(a), _tiles(b)], axis=1).reshape(-1, P, a.shape[0])

    def wide(w):
        t = _tiles(w)
        per = KC // t.shape[2]
        return t.reshape(-1, per, P, t.shape[2], P).transpose(0, 2, 1, 3, 4)

    def long(w):
        t = _tiles(w)
        full = np.zeros((t.shape[0], P, 3 * KC, P), f)
        full[:, :, :t.shape[2]] = t
        return full.reshape(t.shape[0], P, 3, D).transpose(0, 2, 1, 3).reshape(-1, P, D)

    def ffn(gate, up, down):
        put(paired(gate[0], up[0]))
        put(long(down[0]))

    t = _tiles(conv_w_in[0])
    put(np.stack([t[s + c] for c in range(KC) for s in (0, KC, 2 * KC)]))
    put(_tiles(conv_w_out[0]))
    put(wide(ple_w_proj[0]))
    put(_tiles(ple_w_gate[0]))
    t = _tiles(attn_w_in[0])
    put(np.stack([t[n] for c in range(4) for n in [s + 4 * g + c for g in range(3) for s in (0, 12, 24)] + [36 + c]]))
    put(wide(attn_w_out[0]))
    put(wide(ple_w_proj[1]))
    put(_tiles(ple_w_gate[1]))
    ffn(ffn1_w_gate_2, ffn1_w_up_2, ffn1_w_down_2)
    w = w_in_2[0]
    q, kk, v, iq, ik, iw, mx, mv, mi, mf, mo, ga, gb = np.split(
        w, np.cumsum([512, 128, 128, 512, 64, 8, 512, 512, 4, 4, 512, D]), axis=1)
    small = np.zeros((D, P), f)
    small[:, 0:8], small[:, 32:36], small[:, 64:68] = iw, mi, mf
    for part in (small, mx, mv, mo, kk, np.concatenate([ik, ik], axis=1), v):
        put(_tiles(part))
    heads = [64 * h + d for c in range(4) for h in (c, c + 4) for d in range(64)]
    put(_tiles(q[:, heads]))
    put(_tiles(iq))
    for gate, proj in ((gb, w_proj_b_2[0]), (ga, w_proj_a_2[0][heads])):
        g, pr = _tiles(gate), wide(proj)
        for m in range(4):
            put(g[2 * m:2 * m + 2])
            put(pr[m:m + 1])
    put(_tiles(w_out_2[0]))
    ffn(ffn2_w_gate_2, ffn2_w_up_2, ffn2_w_down_2)
    assert at[0] == N_TILES

    params = np.zeros((P, NPARAM), f)

    def param(name, v):
        params[:v.shape[0], PARAMS[name]:PARAMS[name] + v.shape[1]] = v

    param("norm_g0", _cols(norm_g[0]))
    param("norm_g1", _cols(norm_g[1]))
    param("ple_g0", _cols(ple_norm_g[0]))
    param("ple_g1", _cols(ple_norm_g[1]))
    taps = np.concatenate([conv_dw[0], conv_dw_b[0][None]])
    param("taps", taps.reshape(32, KC, P).transpose(2, 1, 0).reshape(P, -1))
    param("ln_g", _cols(conv_ln_g[0]))
    param("ln_b", _cols(conv_ln_b[0]))
    for name, v in (("q_norm", attn_q_norm), ("k_norm", attn_k_norm), ("q_norm2", q_norm_2), ("k_norm2", k_norm_2),
                    ("idx_norm", idx_k_norm_2)):
        param(name, np.concatenate([v[0], v[0]])[:, None])
    param("ffn1", _cols(ffn1_norm_2[0]))
    param("mix", _cols(mix_norm_2[0]))
    param("conv2", conv_w_2[0].reshape(4, 4, P).transpose(2, 1, 0).reshape(P, 16))
    param("conv2_b", _cols(conv_b_2[0]))
    param("m_head", _cols(m_head_norm_2[0]))
    param("ffn2", _cols(ffn2_norm_2[0]))
    param("b_i", b_i_2[0][:, None])
    param("b_f", b_f_2[0][:, None])
    inv = (1.0 / (f(500000.0) ** (np.arange(0, 16, 2, dtype=f) / f(16)))).astype(f)
    freq = np.zeros(HEAD, f)
    freq[0:16] = np.tile(inv, 2)
    param("inv_freq", np.tile(freq, 2)[:, None])
    param("eps", np.full((P, 1), EPS, f))
    param("w_mq", w_mq_2[0].transpose(1, 0, 2).reshape(P, -1))
    param("w_mk", w_mk_2[0].transpose(1, 0, 2).reshape(P, -1))

    r, c = np.arange(P)[:, None], np.arange(P)[None, :]
    rot = np.zeros((P, P), f)
    for h in (0, HEAD):
        for d in range(8):
            rot[h + d + 8, h + d] = -1.0
            rot[h + d, h + d + 8] = 1.0
    pick = np.zeros((P, 4, P), f)
    for h in range(4):
        pick[h, h] = 1.0
    consts = np.concatenate(
        [np.eye(P, dtype=f), np.ones((P, P), f), (r // HEAD == c // HEAD).astype(f), rot,
         np.where((r < 64) & (c >= 64), f(NEG), f(0)), np.where(c < r, f(NEG), f(0)), pick.reshape(P, -1)],
        axis=1).astype(f)

    lq = np.arange(P)[:, None, None]
    res = np.arange(4)[None, :, None]
    key = np.arange(S)[None, None, :]
    dist = 4 * lq + res - key
    near = (dist >= 0) & (dist <= 128)
    lk = np.arange(P)[None, None, :]
    same = np.broadcast_to(lq >= lk, (P, 4, P))
    masks = np.where(np.concatenate([near, same, same & ((lq - lk) % 4 == 0)], axis=2), f(0), f(NEG)).astype(f)
    return {
        "weights": weights,
        "x": np.ascontiguousarray(x[0].reshape(S, KC, P).transpose(2, 1, 0)),
        "ple": np.ascontiguousarray(p[:, 0].reshape(2, S, 2, P).transpose(0, 3, 2, 1)),
        "pos": np.ascontiguousarray(positions),
        "params": params, "consts": consts, "masks": masks,
    }
```
